# Optimizing a Trainium2 kernel written in Bass

```python
import math
import jax, jax.numpy as jnp
from jax import lax
import numpy as np

D_MODEL = 2048
BATCH = 1
SEQ = 512
DEPTH = 1

HEAD_DIM = 128
N_HEADS_TOTAL = D_MODEL // HEAD_DIM
MIX_WIDTH = N_HEADS_TOTAL * HEAD_DIM
N_HEADS_A = (3 * N_HEADS_TOTAL) // 8
N_HEADS_B = N_HEADS_TOTAL // 4
N_HEADS_C = N_HEADS_TOTAL - N_HEADS_A - N_HEADS_B
DIFF_QK_DIM = HEAD_DIM // 2
PROJ_WIDTH = 3 * MIX_WIDTH
DILATED_PATTERNS = ((128, 1), (512, 4), (2048, 16))
DILATED_BLOCK = 128
BLOCK = 128
D_FF = 4 * D_MODEL
NUM_BUCKETS = 32
MAX_DISTANCE = 2048
EPS = 1e-6
NEG_INF = -1e30

kernel_name = "hybrid_dilated_diff_stickbreaking_block"

def rmsnorm(x, g):
    xf = x.astype(jnp.float32)
    y = xf * lax.rsqrt(jnp.mean(xf * xf, axis=-1, keepdims=True) + EPS)
    return y.astype(x.dtype) * g

def t5_bucket(dist):
    n = jnp.maximum(dist, 0)
    max_exact = NUM_BUCKETS // 2
    nf = jnp.maximum(n, max_exact).astype(jnp.float32)
    large = max_exact + (jnp.log(nf / max_exact) / math.log(MAX_DISTANCE / max_exact)
                         * (NUM_BUCKETS - max_exact)).astype(jnp.int32)
    large = jnp.minimum(large, NUM_BUCKETS - 1)
    return jnp.where(n < max_exact, n, large)

def dilated_pattern(q, k, v, table, window, dil):
    B, S, H, D = q.shape
    L = S // dil
    nk = window // dil
    blk = DILATED_BLOCK
    nb = -(-L // blk)
    Lp = nb * blk
    scale = 1.0 / math.sqrt(D)

    def to_strided(t):
        t = jnp.swapaxes(t.reshape(B, L, dil, H, D), 1, 2)
        return jnp.pad(t, ((0, 0), (0, 0), (0, Lp - L), (0, 0), (0, 0)))

    def band(t):
        ts = jnp.pad(to_strided(t), ((0, 0), (0, 0), (blk, 0), (0, 0), (0, 0)))
        ts = ts.reshape(B, dil, nb + 1, blk, H, D)
        return jnp.concatenate([ts[:, :, :-1], ts[:, :, 1:]], axis=3)

    qs = to_strided(q).reshape(B, dil, nb, blk, H, D)
    kb, vb = band(k), band(v)
    i = jnp.arange(blk)[:, None]
    c = jnp.arange(2 * blk)[None, :]
    steps = i + blk - c
    bidx = jnp.arange(nb)[:, None, None]
    valid = (steps >= 0) & (steps <= nk) & (bidx * blk + c - blk >= 0)
    bias = jnp.moveaxis(table[t5_bucket(steps * dil)], -1, 0).astype(jnp.float32)
    logits = jnp.einsum('brnihd,brnchd->brnhic', qs, kb).astype(jnp.float32) * scale + bias
    logits = jnp.where(valid[:, None], logits, NEG_INF)
    lse = jax.nn.logsumexp(logits, axis=-1)
    p = jnp.exp(logits - lse[..., None])
    out = jnp.einsum('brnhic,brnchd->brnihd', p.astype(v.dtype), vb)

    def from_strided(y):
        y = jnp.swapaxes(y[:, :, :L], 1, 2)
        return y.reshape((B, S) + y.shape[3:])

    out = from_strided(out.reshape(B, dil, Lp, H, D))
    lse = from_strided(jnp.swapaxes(lse, 3, 4).reshape(B, dil, Lp, H))
    return out, lse

def dilated_attention(q, k, v, table):
    outs, lses = [], []
    for window, dil in DILATED_PATTERNS:
        o, l = dilated_pattern(q, k, v, table, window, dil)
        outs.append(o)
        lses.append(l)
    w = jax.nn.softmax(jnp.stack(lses), axis=0)
    return jnp.einsum('pbsh,pbshd->bshd', w.astype(q.dtype), jnp.stack(outs))

def diff_attention(q, k, v, table, lam, lam_init, g):
    B, S, H, _, Dq = q.shape
    nb = S // BLOCK
    scale = 1.0 / math.sqrt(Dq)
    qblocks = jnp.moveaxis(q.reshape(B, nb, BLOCK, H, 2, Dq), 1, 0)
    s_pos = jnp.arange(S)

    def one(args):
        qi, bi = args
        t = bi * BLOCK + jnp.arange(BLOCK)
        dist = t[:, None] - s_pos[None, :]
        bias = jnp.moveaxis(table[t5_bucket(dist)], -1, 0).astype(jnp.float32)
        logits = jnp.einsum('bihpd,bshpd->bphis', qi, k).astype(jnp.float32) * scale + bias
        logits = jnp.where(dist >= 0, logits, NEG_INF)
        p = jax.nn.softmax(logits, axis=-1)
        a = p[:, 0] - lam * p[:, 1]
        return jnp.einsum('bhis,bshd->bihd', a.astype(v.dtype), v)

    out = lax.map(one, (qblocks, jnp.arange(nb)))
    out = jnp.moveaxis(out, 0, 1).reshape(B, S, H, v.shape[-1])
    return rmsnorm(out, g) * (1.0 - lam_init)

def stick_breaking_attention(q, k, v):
    B, S, H, D = q.shape
    nb = S // BLOCK
    scale = 1.0 / math.sqrt(D)
    qblocks = jnp.moveaxis(q.reshape(B, nb, BLOCK, H, D), 1, 0)
    s_pos = jnp.arange(S)

    def one(args):
        qi, bi = args
        t = bi * BLOCK + jnp.arange(BLOCK)
        mask = s_pos[None, :] < t[:, None]
        z = jnp.einsum('bihd,bshd->bhis', qi, k).astype(jnp.float32) * scale
        u = jnp.where(mask, jax.nn.log_sigmoid(-z), 0.0)
        r = lax.cumsum(u, axis=3, reverse=True) - u
        a = jnp.where(mask, jnp.exp(jax.nn.log_sigmoid(z) + r), 0.0)
        return jnp.einsum('bhis,bshd->bihd', a.astype(v.dtype), v)

    out = lax.map(one, (qblocks, jnp.arange(nb)))
    return jnp.moveaxis(out, 0, 1).reshape(B, S, H, D)

def setup_inputs(seed: int = 0) -> dict:
    key = jax.random.key(seed)
    ks = jax.random.split(key, 16)
    f32 = jnp.float32
    return {
        "x": jax.random.normal(ks[0], (BATCH, SEQ, D_MODEL), f32),
        "w_in": jax.random.normal(ks[1], (DEPTH, D_MODEL, PROJ_WIDTH), f32) * D_MODEL ** -0.5,
        "w_out": jax.random.normal(ks[2], (DEPTH, MIX_WIDTH, D_MODEL), f32) * MIX_WIDTH ** -0.5,
        "g_attn": 1.0 + 0.02 * jax.random.normal(ks[3], (DEPTH, D_MODEL), f32),
        "g_mlp": 1.0 + 0.02 * jax.random.normal(ks[4], (DEPTH, D_MODEL), f32),
        "w_mlp_in": jax.random.normal(ks[5], (DEPTH, D_MODEL, D_FF), f32) * D_MODEL ** -0.5,
        "w_mlp_out": jax.random.normal(ks[6], (DEPTH, D_FF, D_MODEL), f32) * D_FF ** -0.5,
        "rel_bias_table": 0.5 * jax.random.normal(ks[7], (NUM_BUCKETS, N_HEADS_A + N_HEADS_B), f32),
        "diff_lam_q1": 0.1 * jax.random.normal(ks[8], (DEPTH, DIFF_QK_DIM), f32),
        "diff_lam_k1": 0.1 * jax.random.normal(ks[9], (DEPTH, DIFF_QK_DIM), f32),
        "diff_lam_q2": 0.1 * jax.random.normal(ks[10], (DEPTH, DIFF_QK_DIM), f32),
        "diff_lam_k2": 0.1 * jax.random.normal(ks[11], (DEPTH, DIFF_QK_DIM), f32),
        "diff_subln_g": 1.0 + 0.02 * jax.random.normal(ks[12], (DEPTH, HEAD_DIM), f32),
        "g_final": 1.0 + 0.02 * jax.random.normal(ks[13], (D_MODEL,), f32),
    }

def reference(x, w_in, w_out, g_attn, g_mlp, w_mlp_in, w_mlp_out, rel_bias_table,
              diff_lam_q1, diff_lam_k1, diff_lam_q2, diff_lam_k2, diff_subln_g, g_final):
    B, S, _ = x.shape
    table_a = rel_bias_table[:, :N_HEADS_A]
    table_b = rel_bias_table[:, N_HEADS_A:]
    split_a = 3 * N_HEADS_A * HEAD_DIM
    split_b = split_a + 3 * N_HEADS_B * HEAD_DIM
    for l in range(DEPTH):
        h = rmsnorm(x, g_attn[l])
        proj = h @ w_in[l]
        part_a, part_b, part_c = jnp.split(proj, [split_a, split_b], axis=-1)
        qa, ka, va = [t.reshape(B, S, N_HEADS_A, HEAD_DIM) for t in jnp.split(part_a, 3, axis=-1)]
        qb, kb, vb = jnp.split(part_b, 3, axis=-1)
        qb = qb.reshape(B, S, N_HEADS_B, 2, DIFF_QK_DIM)
        kb = kb.reshape(B, S, N_HEADS_B, 2, DIFF_QK_DIM)
        vb = vb.reshape(B, S, N_HEADS_B, HEAD_DIM)
        qc, kc, vc = [t.reshape(B, S, N_HEADS_C, HEAD_DIM) for t in jnp.split(part_c, 3, axis=-1)]

        lam_init = 0.8 - 0.6 * math.exp(-0.3 * l)
        lam = (jnp.exp(jnp.sum(diff_lam_q1[l].astype(jnp.float32) * diff_lam_k1[l].astype(jnp.float32)))
               - jnp.exp(jnp.sum(diff_lam_q2[l].astype(jnp.float32) * diff_lam_k2[l].astype(jnp.float32)))
               + lam_init)

        out_a = dilated_attention(qa, ka, va, table_a)
        out_b = diff_attention(qb, kb, vb, table_b, lam, lam_init, diff_subln_g[l])
        out_c = stick_breaking_attention(qc, kc, vc)
        mixed = jnp.concatenate([out_a.reshape(B, S, -1), out_b.reshape(B, S, -1),
                                 out_c.reshape(B, S, -1)], axis=-1)
        x = x + mixed @ w_out[l]
        h = rmsnorm(x, g_mlp[l])
        x = x + jnp.square(jax.nn.relu(h @ w_mlp_in[l])) @ w_mlp_out[l]
    return rmsnorm(x, g_final)


_drawn_inputs = setup_inputs


def setup_inputs(seed=0):
    import zlib

    import numpy as np

    out = dict(_drawn_inputs(seed))
    spreads = {}
    factors = {'g_attn': 3.595,
     'g_mlp': 3.411,
     'diff_lam_k1': 8.0,
     'diff_lam_q2': 8.0,
     'diff_subln_g': 8.0,
     'g_final': 2.77}
    for name, (base, spread) in spreads.items():
        noise = np.random.default_rng([zlib.crc32(name.encode()), seed]).standard_normal(out[name].shape)
        drawn = base * np.exp(spread * noise) if base else spread * noise
        out[name] = __import__('jax').numpy.asarray(drawn.astype(out[name].dtype))
    for name, factor in factors.items():
        out[name] = (out[name] * factor).astype(out[name].dtype)
    return out
```

```python
import math
from contextlib import ExitStack

import concourse.bass as bass
from concourse import mybir

F32 = mybir.dt.float32
F32R = mybir.dt.float32r
ACT = mybir.ActivationFunctionType
ALU = mybir.AluOpType
AX_X = mybir.AxisListType.X

P = 128
SEQ = 512
D = 2048
FF = 8192
NT = SEQ // P
NK = D // P
HEADS_A, HEADS_B, HEADS_C = 6, 4, 6
HEADS = HEADS_A + HEADS_B + HEADS_C
GA, GB, GC = 1, 1 + HEADS_A, 1 + HEADS_A + HEADS_B
G_OUT = HEADS
G_MLP = G_OUT + D // 512
CHUNKS = 4
UNIT_W = 512
HEAD_W = 3 * P
AHEAD = 3
SPLIT_RING = 4
EPS = 1e-6
MASKED = -1e30
NUM_BUCKETS, MAX_DISTANCE = 32, 2048
SCALE_AC = 1.0 / math.sqrt(P)
SCALE_B = 1.0 / math.sqrt(P // 2)
LAM_INIT = 0.8 - 0.6 * math.exp(0.0)
VEC = SEQ + P

OFF_Q = [0, 128, 384, 768]
OFF_K = [0, 512, 896, 1152]
PACKED = 1280


def bucket_runs():
    import numpy as np

    half = NUM_BUCKETS // 2
    dist = np.arange(SEQ)
    nf = np.maximum(dist, half).astype(np.float32)
    large = half + (np.log(nf / np.float32(half)) / np.float32(math.log(MAX_DISTANCE / half))
                    * np.float32(NUM_BUCKETS - half)).astype(np.int32)
    bucket = np.where(dist < half, dist, np.minimum(large, NUM_BUCKETS - 1))
    return [(int(b), int(dist[bucket == b][0]), int(dist[bucket == b][-1])) for b in np.unique(bucket)]


VEC_STEPS = 10 + len(bucket_runs())


def build(nc, x, w_in, w_out, g_attn, g_mlp, w_up, w_down, table, lq1, lk1, lq2, lk2, g_sub, g_final, out):
    ctx = ExitStack()
    with ctx:
        def sb(name, shape, dtype=F32):
            return ctx.enter_context(nc.sbuf_tensor(name, shape, dtype))

        def sem(name):
            return ctx.enter_context(nc.semaphore(name))

        raw = sb("raw", [P, 8, UNIT_W])
        w_hi = sb("w_hi", [P, SPLIT_RING, UNIT_W], F32R)
        w_lo = sb("w_lo", [P, SPLIT_RING, UNIT_W], F32R)
        h_hi = sb("h_hi", [P, NK, SEQ], F32R)
        h_lo = sb("h_lo", [P, NK, SEQ], F32R)
        m_hi = sb("m_hi", [P, NK, SEQ], F32R)
        m_lo = sb("m_lo", [P, NK, SEQ], F32R)
        res = sb("res", [P, NT, D])
        flat = res[:, :, :].rearrange("p t c -> p (t c)")
        bias = flat[:, 0:10 * SEQ].rearrange("p (h c) -> p h c", h=10)
        probs_t = flat[:, 5120:5120 + 4 * SEQ].rearrange("p (b i) -> p b i", b=4)
        b_out = flat[:, 7168:7680]
        b_sq = flat[:, 7680:8192]
        attn = sb("attn", [P, 2 * PACKED])
        map0, map1 = attn[:, 0:PACKED], attn[:, PACKED:2 * PACKED]
        v_t = attn[:, PACKED:PACKED + SEQ]
        relu_s = attn[:, 0:4 * SEQ].rearrange("p (b i) -> p b i", b=4)
        g_fin = attn[:, 0:D]
        qT = sb("qT", [P, SEQ])
        kT = sb("kT", [P, SEQ])
        vv = sb("vv", [P, NT, P])
        rstd = sb("rstd", [P, SEQ])
        u_hi = sb("u_hi", [P, PACKED], F32R)
        u_lo = sb("u_lo", [P, PACKED], F32R)
        ident = sb("ident", [P, P])
        ones_r = sb("ones_r", [P, P], F32R)
        ones = ones_r[:, :].bitcast(F32)
        tri_r = sb("tri_r", [P, P], F32R)
        keep = sb("keep", [P, P])
        drop = sb("drop", [P, P])
        small = sb("small", [P, 72])
        ga_col, gm_col = small[:, 0:16], small[:, 16:32]
        gs_col = small[:, 32:33]
        eps_c = small[:, 33:34]
        neg_lam = small[:, 34:35]
        lam_s = small[:, 36:40]
        mx = small[:, 40:48]
        nm = small[:, 48:56]
        sums = small[:, 56:64]
        rec = small[:, 64:72]
        square = kT
        sq_sum = qT
        sq_pair = [vv[:, :, :].rearrange("p b d -> p (b d)"), kT[:, :]]
        vec = map0[0:10, P:P + VEC + NUM_BUCKETS + 1]
        g_rows = map1[0:33, 512:512 + P]
        tab_rows = map1[0:NUM_BUCKETS, 640:650]
        bank = [ctx.enter_context(nc.psum_tensor(f"bank{i}", [P, 512], F32)) for i in range(8)]
        acc = bank[0:4]
        att = bank[4:8]
        tr_bank = [bank[6], bank[3]]
        bias_rows = nc.dram_tensor("bias_rows", [10, P, VEC], F32, kind="Internal")

        s_x = [sem(f"x_chunk{c}_loaded") for c in range(4)]
        s_rowsl = sem("small_rows_loaded")
        s_colT = sem("small_rows_transposed")
        s_small = sem("norm_weights_by_feature")
        s_lamv = sem("lambda_vectors_loaded")
        s_const = sem("constants_made")
        s_tri = sem("triangle_rounded")
        s_raw = [sem(f"raw_quad_slot{i}_loaded") for i in range(2)]
        s_hi = sem("unit_hi_made")
        s_lo = sem("unit_lo_made")
        s_unit = sem("unit_multiplied")
        s_acc = sem("acc_bank_finished_but_the_last")
        s_evac = sem("acc_bank_read")
        s_xt = sem("x_transposed")
        s_hhi = sem("h_hi_made")
        s_sq = sem("square_made")
        s_hlo = sem("h_lo_made")
        s_sqsum = sem("square_added")
        s_ssq = sem("sum_of_squares_in_psum")
        s_root = sem("root_made")
        s_rstd = sem("rstd_made")
        s_tab = sem("bias_table_loaded")
        s_vecb = sem("bias_vector_step")
        s_rows = sem("bias_rows_stored")
        s_bias = sem("bias_loaded")
        s_lam = sem("lambda_step")
        s_lame = sem("lambda_exps")
        s_qkv = sem("qkv_scaled")
        s_vt = sem("v_transposed")
        s_v = sem("v_copied")
        s_aS, s_bS = sem("a_scores"), sem("b_scores")
        s_aL, s_bL = sem("a_logits"), sem("b_logits")
        s_mx = sem("row_max")
        s_nm = sem("negated_max")
        s_e = sem("exps")
        s_r = sem("reciprocal_sums")
        s_rl = sem("second_map_weight")
        s_p0 = sem("first_map_scaled")
        s_p = sem("probs_ready")
        s_pt = sem("probs_transposed")
        s_ptc = sem("probs_transposed_copied")
        s_o = sem("head_out_in_psum")
        s_bo = sem("b_out_copied")
        s_bssq = sem("b_sum_of_squares")
        s_broot = sem("b_root")
        s_bn = sem("b_norm_step")
        s_z = sem("c_scores")
        s_zc = sem("c_logits_copied")
        s_zl = sem("c_log_step")
        s_sp = sem("c_softplus")
        s_spm = sem("c_softplus_masked")
        s_uh = sem("c_softplus_hi")
        s_ul = sem("c_softplus_lo")
        s_rs = sem("c_sums_in_psum")
        s_d = sem("c_exponent")
        s_ca = sem("c_exp")
        s_dm = sem("c_exponent_masked")
        s_mh = sem("mixed_hi_made")
        s_mix = sem("mixed_lo_made")
        s_res = sem("residual_loaded")
        s_relu = sem("relu_made")
        s_rsc = sem("relu_scaled")
        s_rsq = sem("relu_squared")
        s_uhh = sem("hidden_hi_made")
        s_hid = sem("hidden_lo_made")
        s_gfin = sem("g_final_loaded")
        s_fsq = sem("final_sum_of_squares")
        s_froot = sem("final_root")
        s_frec = sem("final_reciprocal")
        s_fx = sem("final_scaled")
        s_fin = sem("final_rows_ready")
        s_out = sem("out_stored")

        def raw_loaded(G, u, after_heads):
            quads = 2 * G + (u // 4) // 2 + 1
            return 16 * quads + 32 * 2 * HEADS if after_heads else 48 * quads

        def banks_done(G, b, after_heads):
            return 4 * G - HEADS + b + 1 if after_heads else 3 * G + b + 1

        def wait_bank(engine, G, b, after_heads):
            if b == (3 if after_heads else 2):
                engine.wait_ge(s_unit, 16 * G + 16)
            else:
                engine.wait_ge(s_acc, 3 * G - HEADS + b + 1 if after_heads else 2 * G + b + 1)

        block = ctx.enter_context(nc.Block())

        @block.sync
        def _(sp):
            x_v = x[0].rearrange("(t p) c -> p t c", p=P)
            in_v = w_in[0].rearrange("(k p) c -> p k c", p=P)
            out_v = w_out[0].rearrange("(k p) c -> p k c", p=P)
            up_v = w_up[0].rearrange("(k p) c -> p k c", p=P)
            down_v = w_down[0].rearrange("(k p) c -> p k c", p=P)
            sp.dma_start(res[:, :, 0:512], x_v[:, :, 0:512]).then_inc(s_x[0], 16)

            def slot_free(G, q):
                sp.wait_ge(s_lo, 16 * G + 4 * q - 4)

            def load_head(G, q, base, heads, h):
                for part in range(3):
                    cols = bass.ds(base + part * heads * P + h * P, P)
                    sp.dma_start(raw[:, 4 * (q % 2):4 * (q % 2) + 4, part * P:part * P + P],
                                 in_v[:, 4 * q:4 * q + 4, cols]).then_inc(s_raw[q % 2], 16)

            for q in range(4):
                if q >= 2:
                    slot_free(0, q)
                load_head(0, q, 0, HEADS_A, 0)
                if q == 2:
                    sp.wait_ge(s_vecb, VEC_STEPS)
                    value = vec[:, 0:VEC].rearrange("h (r n) -> h r n", r=1)
                    sp.dma_start(bias_rows.ap(), value.to_broadcast([10, P, VEC])).then_inc(s_rows, 16)
                if q == 0:
                    for c in range(1, 4):
                        sp.dma_start(res[:, :, 512 * c:512 * c + 512],
                                     x_v[:, :, 512 * c:512 * c + 512]).then_inc(s_x[c], 16)
            for q in range(4):
                slot_free(1, q)
                load_head(1, q, 0, HEADS_A, 1)
                if q == 1:
                    sp.wait_ge(s_rows, 16)
                    sp.wait_ge(s_xt, NK)
                    skewed = bass.AP(tensor=bias_rows, offset=P - 1, ap=[[VEC - 1, P], [P * VEC, 10], [1, SEQ]])
                    sp.dma_start(bias, skewed).then_inc(s_bias, 16)
            with sp.Fori(2, HEADS_A) as h:
                for q in range(4):
                    slot_free(h, q)
                    load_head(h, q, 0, HEADS_A, h)
            with sp.Fori(0, HEADS_B) as h:
                for q in range(4):
                    slot_free(HEADS_A + h, q)
                    load_head(HEADS_A + h, q, 3 * HEADS_A * P, HEADS_B, h)
            first_c = HEADS_A + HEADS_B
            for q in range(4):
                slot_free(first_c, q)
                load_head(first_c, q, 3 * first_c * P, HEADS_C, 0)
            for q in range(4):
                slot_free(first_c + 1, q)
                load_head(first_c + 1, q, 3 * first_c * P, HEADS_C, 1)
            sp.wait_ge(s_mix, first_c)
            sp.dma_start(res[:, :, :], x_v).then_inc(s_res, 16)
            with sp.Fori(2, HEADS_C) as h:
                for q in range(4):
                    slot_free(first_c + h, q)
                    load_head(first_c + h, q, 3 * first_c * P, HEADS_C, h)
            with sp.Fori(0, 4) as g:
                for q in range(4):
                    slot_free(G_OUT + g, q)
                    sp.dma_start(raw[:, 4 * (q % 2):4 * (q % 2) + 4, :],
                                 out_v[:, 4 * q:4 * q + 4, bass.ds(512 * g, 512)]).then_inc(s_raw[q % 2], 16)
            with sp.Fori(0, CHUNKS) as c:
                with sp.Fori(0, 4) as g:
                    for q in range(4):
                        slot_free(G_MLP + 8 * c + g, q)
                        sp.dma_start(raw[:, 4 * (q % 2):4 * (q % 2) + 4, :],
                                     up_v[:, 4 * q:4 * q + 4, bass.ds(2048 * c + 512 * g, 512)])\
                            .then_inc(s_raw[q % 2], 16)
                with sp.Fori(0, 4) as g:
                    for q in range(4):
                        slot_free(G_MLP + 8 * c + 4 + g, q)
                        sp.dma_start(raw[:, 4 * (q % 2):4 * (q % 2) + 4, :],
                                     down_v[:, bass.ds(NK * c + 4 * q, 4), bass.ds(512 * g, 512)])\
                            .then_inc(s_raw[q % 2], 16)
            sp.wait_ge(s_hid, NK * CHUNKS)
            sp.dma_start(g_fin, g_final.rearrange("(o c) -> o c", o=1).to_broadcast([P, D])).then_inc(s_gfin, 16)
            out_t = out[0].rearrange("(t p) c -> p t c", p=P)
            for t in range(NT):
                sp.wait_ge(s_fin, t + 1)
                sp.dma_start(out_t[:, t, :], res[:, t, :]).then_inc(s_out, 16)
            sp.wait_ge(s_out, 16 * NT)

        @block.gpsimd
        def _(pool):
            nc.gpsimd.memset(ident[:, :], 0.0).then_inc(s_const, 1)
            nc.gpsimd.memset(ones, 1.0).then_inc(s_const, 1)
            nc.gpsimd.memset(eps_c, EPS).then_inc(s_const, 1)
            pool.wait_ge(s_const, 3)
            nc.gpsimd.affine_select(out=ident[:, :], in_=ident[:, :], compare_op=ALU.not_equal, fill=1.0,
                                    base=0, pattern=[[-1, P]], channel_multiplier=1).then_inc(s_const, 1)
            nc.gpsimd.affine_select(out=map0[:, 0:P], in_=ones[:, :], compare_op=ALU.is_ge, fill=0.0,
                                    base=0, pattern=[[-1, P]], channel_multiplier=1).then_inc(s_const, 1)

            nc.gpsimd.affine_select(out=keep[:, :], in_=ones[:, :], compare_op=ALU.is_gt, fill=0.0,
                                    base=0, pattern=[[1, P]], channel_multiplier=-1).then_inc(s_const, 1)
            nc.gpsimd.memset(drop[:, :], 0.0).then_inc(s_const, 1)
            pool.wait_ge(s_const, 7)
            nc.gpsimd.affine_select(out=drop[:, :], in_=drop[:, :], compare_op=ALU.is_gt, fill=MASKED,
                                    base=0, pattern=[[1, P]], channel_multiplier=-1).then_inc(s_const, 1)

            value = vec[:, 0:VEC]
            tab = vec[:, VEC:VEC + NUM_BUCKETS]
            inv = vec[:, VEC + NUM_BUCKETS:VEC + NUM_BUCKETS + 1]
            pool.wait_ge(s_tab, 1)
            nc.gpsimd.memset(inv, 1.0 / SCALE_B).then_inc(s_vecb, 1)
            nc.gpsimd.memset(value[:, SEQ:VEC], MASKED).then_inc(s_vecb, 1)
            pool.wait_ge(s_vecb, 2)
            nc.gpsimd.memset(inv[0:HEADS_A, :], 1.0 / SCALE_AC).then_inc(s_vecb, 1)
            runs = bucket_runs()
            for b, lo, hi in runs:
                nc.gpsimd.tensor_copy(value[:, SEQ - 1 - hi:SEQ - lo],
                                      tab[:, b:b + 1].to_broadcast([10, hi - lo + 1])).then_inc(s_vecb, 1)
            step = VEC_STEPS - 7

            def of_distance(first, last, by, rows=HEADS_A):
                a = SEQ - 1 - last
                return value[0:rows, a:SEQ - first:by]

            for first, last, by, add in ((0, 128, 4, math.log(2.0)), (0, 128, 16, math.log(3.0) - math.log(2.0)),
                                         (144, 496, 16, math.log(2.0))):
                pool.wait_ge(s_vecb, step)
                v = of_distance(first, last, by)
                nc.gpsimd.tensor_scalar(v, v, add, None, ALU.add).then_inc(s_vecb, 1)
                step += 1
            pool.wait_ge(s_vecb, step)
            nc.gpsimd.tensor_scalar(value[:, 0:SEQ], value[:, 0:SEQ], inv, None, ALU.mult).then_inc(s_vecb, 1)
            step += 1
            pool.wait_ge(s_vecb, step)
            for rest in (1, 2, 3):
                nc.gpsimd.memset(of_distance(128 + rest, 508 + rest, 4), MASKED).then_inc(s_vecb, 1)
                step += 1
            assert step == VEC_STEPS

            def add_squares(first):
                for n in range(first, first + NK):
                    pool.wait_ge(s_sq, n + 1)
                    if n == first:
                        nc.gpsimd.tensor_copy(sq_sum[:, :], sq_pair[n % 2]).then_inc(s_sqsum, 1)
                    else:
                        pool.wait_ge(s_sqsum, n)
                        nc.gpsimd.tensor_tensor(sq_sum[:, :], sq_sum[:, :], sq_pair[n % 2], ALU.add)\
                            .then_inc(s_sqsum, 1)

            add_squares(0)

            def mask_c(h):
                def softplus_mask(s):
                    for b in C_ITEMS[s]:
                        d = map1[:, OFF_K[b]:OFF_K[b] + P]
                        pool.wait_ge(s_sp, 3 * h + s + 1)
                        nc.gpsimd.tensor_tensor(d, d, keep[:, :], ALU.mult).then_inc(s_spm, 1)

                def exponent_mask(s):
                    for b in C_ITEMS[s]:
                        d = map0[:, OFF_K[b]:OFF_K[b] + P]
                        pool.wait_ge(s_d, 3 * h + s + 1)
                        nc.gpsimd.tensor_tensor(d, d, drop[:, :], ALU.add).then_inc(s_dm, 1)

                softplus_mask(0)
                softplus_mask(1)
                exponent_mask(0)
                softplus_mask(2)
                exponent_mask(1)
                exponent_mask(2)

            pool.wait_ge(s_const, 8)
            with pool.Fori(0, HEADS_C) as h:
                mask_c(h)
            add_squares(NK)

        @block.scalar
        def _(act):
            def split(G, u, width, after_heads):
                if u % 4 == 0:
                    act.wait_ge(s_raw[(u // 4) % 2], raw_loaded(G, u, after_heads))
                if not (isinstance(G, int) and 16 * G + u < SPLIT_RING):
                    act.wait_ge(s_unit, 16 * G + u - SPLIT_RING + 1)
                nc.scalar.activation(w_hi[:, u % SPLIT_RING, 0:width], raw[:, u % 8, 0:width],
                                     ACT.Copy).then_inc(s_hi, 1)

            def norm_block(n, g_col):
                k = n % NK
                act.wait_ge(s_xt, n + 1)
                nc.scalar.activation(h_hi[:, k, :], att[n % 4][:, :], ACT.Copy, scale=g_col[:, k:k + 1])\
                    .then_inc(s_hhi, 1)
                if n % NK >= 2:
                    act.wait_ge(s_sqsum, n - 1)
                nc.scalar.activation(sq_pair[n % 2], att[n % 4][:, :], ACT.Square).then_inc(s_sq, 1)

            def norm_root(n):
                act.wait_ge(s_ssq, n + 1)
                nc.scalar.activation(rstd[:, :], att[3][:, :], ACT.Sqrt, bias=eps_c, scale=1.0 / D)\
                    .then_inc(s_root, 1)

            act.dma_start(g_rows[0:16, :], g_attn[0].rearrange("(k p) -> k p", p=P)).then_inc(s_rowsl, 16)
            act.dma_start(g_rows[16:32, :], g_mlp[0].rearrange("(k p) -> k p", p=P)).then_inc(s_rowsl, 16)
            act.dma_start(g_rows[32:33, :], g_sub).then_inc(s_rowsl, 16)
            act.dma_start(tab_rows, table).then_inc(s_rowsl, 16)
            for i, v in enumerate((lq1, lk1, lq2, lk2)):
                act.dma_start(b_lam(map1, i), v.to_broadcast([P, P // 2])).then_inc(s_lamv, 16)
            act.wait_ge(s_colT, 1)
            nc.scalar.activation(small[:, 0:33], att[3][:, 0:33], ACT.Copy).then_inc(s_small, 1)
            nc.scalar.activation(vec[:, VEC:VEC + NUM_BUCKETS], att[3][0:10, 64:64 + NUM_BUCKETS], ACT.Copy)\
                .then_inc(s_tab, 1)
            act.wait_ge(s_const, 5)
            nc.scalar.activation(tri_r[:, :], map0[:, 0:P], ACT.Copy).then_inc(s_tri, 1)
            act.wait_ge(s_lam, 4)
            nc.scalar.activation(lam_s[:, 2:4], lam_s[:, 0:2], ACT.Exp).then_inc(s_lame, 1)
            act.wait_ge(s_small, 1)
            for u in range(AHEAD):
                norm_block(u, ga_col)
                split(0, u, HEAD_W, False)
            for u in range(NK):
                if u + AHEAD < NK:
                    norm_block(u + AHEAD, ga_col)
                split(0, u + AHEAD, HEAD_W, False)
                if u == NK - 1:
                    norm_root(0)

            def copy_v(head):
                act.wait_ge(s_vt, head + 1)
                nc.scalar.activation(vv[:, :, :].rearrange("p b d -> p (b d)"), att[3][:, :], ACT.Copy)\
                    .then_inc(s_v, 1)

            def copy_probs(count, b):
                act.wait_ge(s_pt, count)
                nc.scalar.activation(probs_t[:, 0:b + 1, b * P:b * P + P],
                                     tr_bank[b % 2][:, 0:P * (b + 1)].rearrange("p (k i) -> p k i", i=P),
                                     ACT.Copy).then_inc(s_ptc, 1)

            def exp_rows(count, b, m, scale):
                rows = (map0, map1)[m][:, OFF_Q[b]:OFF_Q[b] + P * (b + 1)]
                c = 2 * b + m
                act.wait_ge(s_nm, count)
                nc.scalar.activation(rows, rows, ACT.Exp, bias=nm[:, c:c + 1], scale=scale,
                                     accum_out=sums[:, c:c + 1]).then_inc(s_e, 1)

            with act.Fori(0, HEADS_A) as h:
                for u in range(NK):
                    split(GA + h, u + AHEAD, HEAD_W, False)
                    if u == 1:
                        copy_v(h)
                    if 1 <= u <= 4:
                        exp_rows(4 * h + u, u - 1, 0, SCALE_AC)
                    if u in (5, 6, 7, 9):
                        b = (5, 6, 7, 9).index(u)
                        copy_probs(4 * h + b + 1, b)
            with act.Fori(0, HEADS_B) as h:
                for u in range(NK):
                    split(GB + h, u + AHEAD, HEAD_W, False)
                    if u == 1:
                        copy_v(HEADS_A + h)
                    if u in (2, 4, 6, 8):
                        b = u // 2 - 1
                        for m in range(2):
                            exp_rows(4 * HEADS_A + 8 * h + 2 * b + m + 1, b, m, SCALE_B)
                    if u in (5, 7, 9, 11):
                        b = (u - 5) // 2
                        copy_probs(4 * (HEADS_A + h) + b + 1, b)
                    if u == 13:
                        act.wait_ge(s_o, HEADS_A + h + 1)
                        nc.scalar.activation(b_sq, att[3][:, :], ACT.Square).then_inc(s_bo, 1)
                        nc.scalar.activation(b_out, att[3][:, :], ACT.Copy).then_inc(s_bo, 1)
                    if u == 15:
                        act.wait_ge(s_bssq, h + 1)
                        nc.scalar.activation(b_sq, att[0][:, :], ACT.Sqrt, bias=eps_c, scale=1.0 / P)\
                            .then_inc(s_broot, 1)

            def attend_c(u, h):
                if u == 1:
                    copy_v(HEADS_A + HEADS_B + h)
                if u in (1, 3, 5):
                    s = u // 2
                    lo, n = C_SPAN[s]
                    t = map1[:, lo:lo + n]
                    act.wait_ge(s_z, 3 * h + s + 1)
                    nc.scalar.activation(t, att[C_BANK[s]][:, 0:n], ACT.Abs, scale=SCALE_AC).then_inc(s_zl, 1)
                    nc.scalar.activation(map0[:, lo:lo + n], att[C_BANK[s]][:, 0:n], ACT.Copy,
                                         scale=SCALE_AC).then_inc(s_zc, 1)
                    act.wait_ge(s_zl, 9 * h + 3 * s + 1)
                    nc.scalar.activation(t, t, ACT.Exp, scale=-1.0).then_inc(s_zl, 1)
                    act.wait_ge(s_zl, 9 * h + 3 * s + 2)
                    nc.scalar.activation(t, t, ACT.Ln, bias=1.0).then_inc(s_zl, 1)
                if u in (6, 8, 10):
                    s = (u - 6) // 2
                    lo, n = C_SPAN[s]
                    act.wait_ge(s_dm, 4 * h + C_BLOCKS_DONE[s])
                    nc.scalar.activation(map0[:, lo:lo + n], map0[:, lo:lo + n], ACT.Exp).then_inc(s_ca, 1)

            with act.Fori(0, HEADS_C - 2) as h:
                for u in range(NK):
                    split(GC + h, u + AHEAD, HEAD_W, False)
                    attend_c(u, h)
            for h in (HEADS_C - 2, HEADS_C - 1):
                for u in range(NK):
                    late = GC + h >= G_OUT or u + AHEAD >= NK
                    split(GC + h, u + AHEAD, UNIT_W if late else HEAD_W, late)
                    attend_c(u, h)
            for G in range(G_OUT + 1, G_MLP + 1):
                for u in range(NK):
                    split(G, u + AHEAD, UNIT_W, True)
                    if 1 <= u <= 4:
                        norm_block(NK + 4 * (G - G_OUT - 1) + u - 1, gm_col)
                    if G == G_MLP and u == 8:
                        norm_root(1)

            def relu_bank(G, b):
                wait_bank(act, G, b, True)
                nc.scalar.activation(relu_s[:, b, :], acc[b][:, :], ACT.Relu).then_inc(s_evac, 1)

            def square_relu(n):
                act.wait_ge(s_rsc, n + 1)

            def up_tail(G, c, g, next_splits=True):
                first = 16 * c + 4 * g
                for b in range(4):
                    relu_bank(G, b)
                for b in range(4):
                    act.wait_ge(s_rsc, first + b + 1)
                    if b >= 2:
                        act.wait_ge(s_hid, first + b - 1)
                    nc.scalar.activation((qT, kT)[b % 2][:, :], relu_s[:, b, :], ACT.Square).then_inc(s_rsq, 1)

            def units(G, last=False):
                for u in range(NK):
                    if not (last and u + AHEAD >= NK):
                        split(G, u + AHEAD, UNIT_W, True)

            up_tail(G_MLP, 0, 0)
            with act.Fori(1, 4) as g:
                units(G_MLP + g)
                up_tail(G_MLP + g, 0, g)
            with act.Fori(4, 8) as g:
                units(G_MLP + g)
            with act.Fori(1, CHUNKS - 1) as c:
                with act.Fori(0, 4) as g:
                    units(G_MLP + 8 * c + g)
                    up_tail(G_MLP + 8 * c + g, c, g)
                with act.Fori(4, 8) as g:
                    units(G_MLP + 8 * c + g)
            c = CHUNKS - 1
            with act.Fori(0, 4) as g:
                units(G_MLP + 8 * c + g)
                up_tail(G_MLP + 8 * c + g, c, g)
            with act.Fori(4, 7) as g:
                units(G_MLP + 8 * c + g)
            units(G_MLP + 8 * c + 7, last=True)
            for t in range(NT):
                act.wait_ge(s_evac, banks_done(G_MLP + 8 * c + 7, t, True))
                nc.scalar.activation(h_lo[:, 4 * t:4 * t + 4, :].rearrange("p a b -> p (a b)"), res[:, t, :],
                                     ACT.Square, accum_out=sums[:, t:t + 1]).then_inc(s_fsq, 1)
            act.wait_ge(s_fsq, NT)
            nc.scalar.activation(nm[:, 0:NT], sums[:, 0:NT], ACT.Sqrt, bias=eps_c, scale=1.0 / D)\
                .then_inc(s_froot, 1)
            act.wait_ge(s_frec, 1)
            for t in range(NT):
                nc.scalar.activation(res[:, t, :], res[:, t, :], ACT.Copy, scale=rec[:, t:t + 1]).then_inc(s_fx, 1)

        @block.vector
        def _(dve):
            def split(G, u, width):
                dve.wait_ge(s_hi, 16 * G + u + 1)
                nc.vector.tensor_tensor(w_lo[:, u % SPLIT_RING, 0:width], raw[:, u % 8, 0:width],
                                        w_hi[:, u % SPLIT_RING, 0:width].bitcast(F32), ALU.subtract)\
                    .then_inc(s_lo, 1)

            def norm_block(n, g_col):
                k = n % NK
                dve.wait_ge(s_sq, n + 1)
                nc.vector.scalar_tensor_tensor(h_lo[:, k, :], att[n % 4][:, :], g_col[:, k:k + 1],
                                               h_hi[:, k, :].bitcast(F32), ALU.mult, ALU.subtract)\
                    .then_inc(s_hlo, 1)

            def norm_rstd(n):
                dve.wait_ge(s_root, n + 1)
                nc.vector.reciprocal(rstd[:, :], rstd[:, :]).then_inc(s_rstd, 1)

            def read_head(G):
                for b, dst in enumerate((qT[:, :], kT[:, :], v_t)):
                    wait_bank(dve, G, b, False)
                    nc.vector.tensor_tensor(dst, acc[b][:, :], rstd[:, :], ALU.mult).then_inc(s_evac, 1)

            dve.wait_ge(s_lamv, 64)
            for i in range(2):
                nc.vector.tensor_tensor(b_lam(map1, 2 * i), b_lam(map1, 2 * i), b_lam(map1, 2 * i + 1), ALU.mult)\
                    .then_inc(s_lam, 1)
            dve.wait_ge(s_lam, 2)
            for i in range(2):
                nc.vector.reduce_sum(lam_s[:, i:i + 1], b_lam(map1, 2 * i), AX_X).then_inc(s_lam, 1)
            dve.wait_ge(s_lame, 1)
            nc.vector.scalar_tensor_tensor(neg_lam, lam_s[:, 2:3], -1.0, lam_s[:, 3:4], ALU.mult, ALU.add)\
                .then_inc(s_lam, 1)
            dve.wait_ge(s_lam, 5)
            nc.vector.tensor_scalar(neg_lam, neg_lam, -LAM_INIT, None, ALU.add).then_inc(s_lam, 1)
            dve.wait_ge(s_small, 1)
            nc.vector.tensor_scalar(gs_col, gs_col, 1.0 - LAM_INIT, None, ALU.mult).then_inc(s_lam, 1)

            for u in range(AHEAD):
                norm_block(u, ga_col)
                split(0, u, HEAD_W)
            for u in range(NK):
                if u + AHEAD < NK:
                    norm_block(u + AHEAD, ga_col)
                split(0, u + AHEAD, HEAD_W)
            norm_rstd(0)
            dve.wait_ge(s_rstd, 1)
            read_head(0)

            def logits(scores_sem, scores_count, logits_sem, head, count, b, m, psum, scale):
                n = P * (b + 1)
                rows = (map0, map1)[m][:, OFF_Q[b]:OFF_Q[b] + n]
                c = 2 * b + m
                dve.wait_ge(scores_sem, scores_count)
                nc.vector.tensor_tensor(rows, psum[:, 0:n],
                                        bias[:, bass.ds(head, 1), SEQ - n:SEQ].rearrange("p o c -> p (o c)"),
                                        ALU.add).then_inc(logits_sem, 1)
                return rows, c

            def row_max(logits_sem, logits_count, rows, c, count, scale):
                dve.wait_ge(logits_sem, logits_count)
                nc.vector.reduce_max(mx[:, c:c + 1], rows, AX_X).then_inc(s_mx, 1)
                dve.wait_ge(s_mx, count)
                nc.vector.tensor_scalar(nm[:, c:c + 1], mx[:, c:c + 1], -scale, None, ALU.mult).then_inc(s_nm, 1)

            def mixed(head, src, count):
                hi = m_hi[:, bass.ds(head, 1), :].rearrange("p o c -> p (o c)")
                lo = m_lo[:, bass.ds(head, 1), :].rearrange("p o c -> p (o c)")
                nc.vector.tensor_scalar(hi, src, 1.0, None, ALU.mult).then_inc(s_mh, 1)
                dve.wait_ge(s_mh, count)
                nc.vector.tensor_tensor(lo, src, hi.bitcast(F32), ALU.subtract).then_inc(s_mix, 1)

            dve.wait_ge(s_bias, 16)
            with dve.Fori(0, HEADS_A) as h:
                for u in range(NK):
                    split(GA + h, u + AHEAD, HEAD_W)
                    if 1 <= u <= 4:
                        b = u - 1
                        rows, c = logits(s_aS, 4 * h + u, s_aL, h, 4 * h + u, b, 0, att[b % 2], SCALE_AC)
                        row_max(s_aL, 4 * h + u, rows, c, 4 * h + u, SCALE_AC)
                    if 2 <= u <= 5:
                        b = u - 2
                        dve.wait_ge(s_e, 4 * h + b + 1)
                        nc.vector.reciprocal(rec[:, 2 * b:2 * b + 1], sums[:, 2 * b:2 * b + 1]).then_inc(s_r, 1)
                        dve.wait_ge(s_r, 4 * h + b + 1)
                        rows = map0[:, OFF_Q[b]:OFF_Q[b] + P * (b + 1)]
                        nc.vector.tensor_scalar(rows, rows, rec[:, 2 * b:2 * b + 1], None, ALU.mult)\
                            .then_inc(s_p, 1)
                    if u == 11:
                        dve.wait_ge(s_o, h + 1)
                        mixed(h, att[3][:, :], h + 1)
                read_head(GA + h)
            with dve.Fori(0, HEADS_B) as h:
                n0 = 4 * HEADS_A + 8 * h
                for u in range(NK):
                    split(GB + h, u + AHEAD, HEAD_W)
                    if u in (1, 3, 5, 7):
                        b = u // 2
                        pair = [logits(s_bS, 8 * h + 2 * b + m + 1, s_bL, HEADS_A + h, 0, b, m, att[m], SCALE_B)
                                for m in range(2)]
                        for m, (rows, c) in enumerate(pair):
                            row_max(s_bL, 8 * h + 2 * b + m + 1, rows, c, n0 + 2 * b + m + 1, SCALE_B)
                    if u in (3, 5, 7, 9):
                        b = (u - 3) // 2
                        c = 2 * b
                        dve.wait_ge(s_e, n0 + 2 * b + 2)
                        nc.vector.reciprocal(rec[:, c:c + 2], sums[:, c:c + 2]).then_inc(s_r, 1)
                        dve.wait_ge(s_r, 4 * (HEADS_A + h) + b + 1)
                        rows0 = map0[:, OFF_Q[b]:OFF_Q[b] + P * (b + 1)]
                        rows1 = map1[:, OFF_Q[b]:OFF_Q[b] + P * (b + 1)]
                        nc.vector.tensor_scalar(rec[:, c + 1:c + 2], rec[:, c + 1:c + 2], neg_lam, None, ALU.mult)\
                            .then_inc(s_rl, 1)
                        nc.vector.tensor_scalar(rows0, rows0, rec[:, c:c + 1], None, ALU.mult).then_inc(s_p0, 1)
                        dve.wait_ge(s_rl, 4 * h + b + 1)
                        dve.wait_ge(s_p0, 4 * h + b + 1)
                        nc.vector.scalar_tensor_tensor(rows0, rows1, rec[:, c + 1:c + 2], rows0, ALU.mult, ALU.add)\
                            .then_inc(s_p, 1)
                dve.wait_ge(s_broot, h + 1)
                nc.vector.reciprocal(b_sq, b_sq).then_inc(s_bn, 1)
                dve.wait_ge(s_bn, 2 * h + 1)
                nc.vector.scalar_tensor_tensor(b_out, b_out, gs_col, b_sq, ALU.mult, ALU.mult).then_inc(s_bn, 1)
                dve.wait_ge(s_bn, 2 * h + 2)
                mixed(HEADS_A + h, b_out, HEADS_A + h + 1)
                read_head(GB + h)

            def attend_c(u, h, head):
                if u in (3, 5, 7):
                    s = (u - 3) // 2
                    lo, n = C_SPAN[s]
                    dve.wait_ge(s_zl, 9 * h + 3 * s + 3)
                    dve.wait_ge(s_zc, 3 * h + s + 1)
                    nc.vector.scalar_tensor_tensor(map1[:, lo:lo + n], map0[:, lo:lo + n], 0.0, map1[:, lo:lo + n],
                                                   ALU.max, ALU.add).then_inc(s_sp, 1)
                if u in (4, 6, 8):
                    s = (u - 4) // 2
                    lo, n = C_SPAN[s]
                    dve.wait_ge(s_spm, 4 * h + C_BLOCKS_DONE[s])
                    nc.vector.tensor_scalar(u_hi[:, lo:lo + n], map1[:, lo:lo + n], 1.0, None, ALU.mult)\
                        .then_inc(s_uh, 1)
                    dve.wait_ge(s_uh, 3 * h + s + 1)
                    nc.vector.tensor_tensor(u_lo[:, lo:lo + n], map1[:, lo:lo + n],
                                            u_hi[:, lo:lo + n].bitcast(F32), ALU.subtract).then_inc(s_ul, 1)
                if u in (6, 8, 10):
                    s = (u - 6) // 2
                    lo, n = C_SPAN[s]
                    dve.wait_ge(s_rs, 3 * h + s + 1)
                    nc.vector.tensor_tensor(map0[:, lo:lo + n], map0[:, lo:lo + n], att[C_BANK[s]][:, 0:n],
                                            ALU.subtract).then_inc(s_d, 1)
                if u == 13:
                    dve.wait_ge(s_o, head + 1)
                    mixed(head, att[3][:, :], head + 1)

            with dve.Fori(0, HEADS_C - 2) as h:
                for u in range(NK):
                    split(GC + h, u + AHEAD, HEAD_W)
                    attend_c(u, h, HEADS_A + HEADS_B + h)
                read_head(GC + h)
            for h in (HEADS_C - 2, HEADS_C - 1):
                for u in range(NK):
                    late = GC + h >= G_OUT or u + AHEAD >= NK
                    split(GC + h, u + AHEAD, UNIT_W if late else HEAD_W)
                    attend_c(u, h, HEADS_A + HEADS_B + h)
                if h == HEADS_C - 2:
                    read_head(GC + h)

            def add_residual(G, g):
                for t in range(NT):
                    r = res[:, t, bass.ds(512 * g, 512)]
                    wait_bank(dve, G, t, True)
                    nc.vector.tensor_tensor(r, r, acc[t][:, :], ALU.add).then_inc(s_evac, 1)

            dve.wait_ge(s_res, 16)
            add_residual(G_OUT, 0)
            for G in range(G_OUT + 1, G_MLP + 1):
                for u in range(NK):
                    split(G, u + AHEAD, UNIT_W)
                    if 1 <= u <= 4:
                        norm_block(NK + 4 * (G - G_OUT - 1) + u - 1, gm_col)
                if G < G_MLP:
                    add_residual(G, G - G_OUT)
            norm_rstd(1)
            dve.wait_ge(s_rstd, 2)

            def up_tail(c, g):
                first = 16 * c + 4 * g
                for b in range(4):
                    dve.wait_ge(s_relu_like, relu_count(c, g, b))
                    nc.vector.tensor_tensor(relu_s[:, b, :], relu_s[:, b, :], rstd[:, :], ALU.mult)\
                        .then_inc(s_rsc, 1)
                for b in range(4):
                    hi = m_hi[:, bass.ds(4 * g + b, 1), :].rearrange("p o c -> p (o c)")
                    lo = m_lo[:, bass.ds(4 * g + b, 1), :].rearrange("p o c -> p (o c)")
                    dve.wait_ge(s_rsc, first + b + 1)
                    nc.vector.tensor_tensor(hi, relu_s[:, b, :], relu_s[:, b, :], ALU.mult).then_inc(s_uhh, 1)
                    dve.wait_ge(s_uhh, first + b + 1)
                    dve.wait_ge(s_rsq, first + b + 1)
                    nc.vector.tensor_tensor(lo, (qT, kT)[b % 2][:, :], hi.bitcast(F32), ALU.subtract)\
                        .then_inc(s_hid, 1)

            s_relu_like = s_evac

            def relu_count(c, g, b):
                return banks_done(G_MLP + 8 * c + g, b, True)

            def units(G, last=False):
                for u in range(NK):
                    if not (last and u + AHEAD >= NK):
                        split(G, u + AHEAD, UNIT_W)

            up_tail(0, 0)
            with dve.Fori(1, 4) as g:
                units(G_MLP + g)
                up_tail(0, g)
            with dve.Fori(0, 4) as g:
                units(G_MLP + 4 + g)
                add_residual(G_MLP + 4 + g, g)
            with dve.Fori(1, CHUNKS - 1) as c:
                with dve.Fori(0, 4) as g:
                    units(G_MLP + 8 * c + g)
                    up_tail(c, g)
                with dve.Fori(0, 4) as g:
                    units(G_MLP + 8 * c + 4 + g)
                    add_residual(G_MLP + 8 * c + 4 + g, g)
            c = CHUNKS - 1
            with dve.Fori(0, 4) as g:
                units(G_MLP + 8 * c + g)
                up_tail(c, g)
            with dve.Fori(0, 3) as g:
                units(G_MLP + 8 * c + 4 + g)
                add_residual(G_MLP + 8 * c + 4 + g, g)
            units(G_MLP + 8 * c + 7, last=True)
            add_residual(G_MLP + 8 * c + 7, 3)
            dve.wait_ge(s_froot, 1)
            nc.vector.reciprocal(rec[:, 0:NT], nm[:, 0:NT]).then_inc(s_frec, 1)
            dve.wait_ge(s_gfin, 16)
            for t in range(NT):
                dve.wait_ge(s_fx, t + 1)
                nc.vector.tensor_tensor(res[:, t, :], res[:, t, :], g_fin, ALU.mult).then_inc(s_fin, 1)

        @block.tensor
        def _(pe):
            def mm(o, a, b, start, stop=True):
                return nc.tensor.matmul(o, a, b, start=start, stop=stop, skip_group_check=True)

            def head_unit(G, u):
                s = u % SPLIT_RING
                pe.wait_ge(s_lo, 16 * G + u + 1)
                for b in range(3):
                    cols = slice(b * P, b * P + P)
                    if u == 0 and not (isinstance(G, int) and G == 0):
                        pe.wait_ge(s_evac, banks_done(G - 1, b, False))
                    mm(acc[b][:, :], w_hi[:, s, cols], h_hi[:, u, :], start=(u == 0))
                    mm(acc[b][:, :], w_hi[:, s, cols], h_lo[:, u, :], start=False)
                    last = mm(acc[b][:, :], w_lo[:, s, cols], h_hi[:, u, :], start=False)
                    if u == NK - 1 and b < 2:
                        last.then_inc(s_acc, 1)
                last.then_inc(s_unit, 1)

            def by_token_unit(G, u, prev_after_heads=True):
                s = u % SPLIT_RING
                pe.wait_ge(s_lo, 16 * G + u + 1)
                for t in range(NT):
                    toks = slice(t * P, t * P + P)
                    if u == 0:
                        if prev_after_heads:
                            pe.wait_ge(s_evac, banks_done(G - 1, t, True))
                        elif t < 3:
                            pe.wait_ge(s_evac, banks_done(G - 1, t, False))
                    mm(acc[t][:, :], m_hi[:, u, toks], w_hi[:, s, :], start=(u == 0))
                    mm(acc[t][:, :], m_hi[:, u, toks], w_lo[:, s, :], start=False)
                    last = mm(acc[t][:, :], m_lo[:, u, toks], w_hi[:, s, :], start=False)
                    if u == NK - 1 and t < 3:
                        last.then_inc(s_acc, 1)
                last.then_inc(s_unit, 1)

            def up_unit(G, u):
                s = u % SPLIT_RING
                pe.wait_ge(s_lo, 16 * G + u + 1)
                for b in range(4):
                    cols = slice(b * P, b * P + P)
                    if u == 0:
                        pe.wait_ge(s_evac, banks_done(G - 1, b, True))
                    mm(acc[b][:, :], w_hi[:, s, cols], h_hi[:, u, :], start=(u == 0))
                    mm(acc[b][:, :], w_hi[:, s, cols], h_lo[:, u, :], start=False)
                    last = mm(acc[b][:, :], w_lo[:, s, cols], h_hi[:, u, :], start=False)
                    if u == NK - 1 and b < 3:
                        last.then_inc(s_acc, 1)
                last.then_inc(s_unit, 1)

            def transpose_x(n):
                k = n % NK
                if n < NK and k % 4 == 0:
                    pe.wait_ge(s_x[k // 4], 16)
                if n >= NK:
                    G = G_OUT + (n - NK) // 4
                    pe.wait_ge(s_evac, banks_done(G, 3, True))
                if n >= 4:
                    pe.wait_ge(s_hlo, n - 3)
                if n == 3:
                    pe.wait_ge(s_tab, 1)
                for t in range(NT):
                    last = nc.tensor.transpose(att[n % 4][:, t * P:t * P + P], res[:, t, k * P:k * P + P],
                                               ident[:, :])
                last.then_inc(s_xt, 1)

            def sum_squares(n):
                pe.wait_ge(s_sqsum, NK * (n + 1))
                pe.wait_ge(s_hlo, NK * (n + 1))
                mm(att[3][:, :], ones[:, :], sq_sum[:, :], start=True).then_inc(s_ssq, 1)

            pe.wait_ge(s_const, 5)
            pe.wait_ge(s_rowsl, 64)
            nc.tensor.transpose(att[3][:, 0:33], g_rows, ident[0:33, 0:33])
            nc.tensor.transpose(att[3][0:10, 64:64 + NUM_BUCKETS], tab_rows,
                                ident[0:NUM_BUCKETS, 0:NUM_BUCKETS]).then_inc(s_colT, 1)
            for n in range(AHEAD):
                transpose_x(n)
            for u in range(NK):
                pe.wait_ge(s_hlo, u + 1)
                head_unit(0, u)
                if u + AHEAD < NK:
                    transpose_x(u + AHEAD)
                if u == NK - 2:
                    sum_squares(0)

            def transpose_v(head):
                pe.wait_ge(s_evac, 3 * head + 3)
                for b in range(NT):
                    last = nc.tensor.transpose(att[3][:, b * P:b * P + P], v_t[:, b * P:b * P + P], ident[:, :])
                last.then_inc(s_vt, 1)

            def transpose_probs(head, b):
                pe.wait_ge(s_p, 4 * head + b + 1)
                if b >= 2:
                    pe.wait_ge(s_ptc, 4 * head + b - 1)
                for k in range(b + 1):
                    last = nc.tensor.transpose(tr_bank[b % 2][:, k * P:k * P + P],
                                               map0[:, OFF_Q[b] + k * P:OFF_Q[b] + k * P + P], ident[:, :])
                last.then_inc(s_pt, 1)

            def head_out(head):
                pe.wait_ge(s_ptc, 4 * head + 4)
                pe.wait_ge(s_v, head + 1)
                for b in range(NT):
                    last = mm(att[3][:, b * P:SEQ], vv[:, b, :], probs_t[:, b, b * P:SEQ], start=(b == 0))
                last.then_inc(s_o, 1)

            with pe.Fori(0, HEADS_A) as h:
                for u in range(NK):
                    head_unit(GA + h, u)
                    if u == 0:
                        transpose_v(h)
                    if u <= 3:
                        if u >= 2:
                            pe.wait_ge(s_aL, 4 * h + u - 1)
                        mm(att[u % 2][:, 0:P * (u + 1)], qT[:, u * P:u * P + P], kT[:, 0:P * (u + 1)],
                           start=True).then_inc(s_aS, 1)
                    if u in (4, 5, 6, 8):
                        transpose_probs(h, (4, 5, 6, 8).index(u))
                    if u == 10:
                        head_out(h)
            with pe.Fori(0, HEADS_B) as h:
                for u in range(NK):
                    head_unit(GB + h, u)
                    if u == 0:
                        transpose_v(HEADS_A + h)
                    if u in (0, 2, 4, 6):
                        b = u // 2
                        for m in range(2):
                            if b >= 1:
                                pe.wait_ge(s_bL, 8 * h + 2 * b + m - 1)
                            half = slice(m * (P // 2), (m + 1) * (P // 2))
                            mm(att[m][:, 0:P * (b + 1)], qT[half, b * P:b * P + P], kT[half, 0:P * (b + 1)],
                               start=True).then_inc(s_bS, 1)
                    if u in (4, 6, 8, 10):
                        transpose_probs(HEADS_A + h, (u - 4) // 2)
                    if u == 12:
                        head_out(HEADS_A + h)
                    if u == 14:
                        pe.wait_ge(s_bo, 2 * h + 1)
                        mm(att[0][:, :], ones[:, :], b_sq, start=True).then_inc(s_bssq, 1)

            def attend_c(u, h, head):
                if u == 0:
                    transpose_v(head)
                    for s, blocks in enumerate(C_ITEMS):
                        for j, b in enumerate(blocks):
                            o = OFF_K[b] - C_SPAN[s][0]
                            last = mm(att[C_BANK[s]][:, o:o + SEQ - b * P], kT[:, b * P:b * P + P],
                                      qT[:, b * P:SEQ], start=True)
                        last.then_inc(s_z, 1)
                if u in (5, 7, 9):
                    s = (u - 5) // 2
                    pe.wait_ge(s_ul, 3 * h + s + 1)
                    first = True
                    for b in C_ITEMS[s]:
                        o = OFF_K[b] - C_SPAN[s][0]
                        for later in range(b, NT):
                            weight = tri_r if later == b else ones_r
                            skip = (later - b) * P
                            for part in (u_hi, u_lo):
                                last = mm(att[C_BANK[s]][:, o + skip:o + SEQ - b * P], weight[:, :],
                                          part[:, OFF_K[later]:OFF_K[later] + SEQ - later * P], start=first)
                                first = False
                    last.then_inc(s_rs, 1)
                if u == 12:
                    pe.wait_ge(s_ca, 3 * h + 3)
                    pe.wait_ge(s_v, head + 1)
                    for b in range(NT):
                        last = mm(att[3][:, b * P:SEQ], vv[:, b, :], map0[:, OFF_K[b]:OFF_K[b] + SEQ - b * P],
                                  start=(b == 0))
                    last.then_inc(s_o, 1)

            pe.wait_ge(s_tri, 1)
            with pe.Fori(0, HEADS_C - 1) as h:
                for u in range(NK):
                    head_unit(GC + h, u)
                    attend_c(u, h, HEADS_A + HEADS_B + h)
            for u in range(NK):
                if u == NK - 1:
                    pe.wait_ge(s_mix, HEADS)
                by_token_unit(G_OUT, u, prev_after_heads=False)
                attend_c(u, HEADS_C - 1, HEADS - 1)
            for G in range(G_OUT + 1, G_MLP):
                for u in range(NK):
                    by_token_unit(G, u)
                    if u < 4:
                        transpose_x(NK + 4 * (G - G_OUT - 1) + u)
            for u in range(NK):
                if u >= NK - 4:
                    pe.wait_ge(s_hlo, NK + u + 1)
                if u == 0:
                    pe.wait_ge(s_hlo, 2 * NK - 4)
                up_unit(G_MLP, u)
                if u < 4:
                    transpose_x(2 * NK - 4 + u)
                if u == 7:
                    sum_squares(1)
            with pe.Fori(1, 4) as g:
                for u in range(NK):
                    up_unit(G_MLP + g, u)

            def down(c, g):
                for u in range(NK):
                    if u % 4 == 0:
                        pe.wait_ge(s_hid, NK * c + u + 4)
                    by_token_unit(G_MLP + 8 * c + 4 + g, u)

            with pe.Fori(0, 4) as g:
                down(0, g)
            with pe.Fori(1, CHUNKS) as c:
                with pe.Fori(0, 4) as g:
                    for u in range(NK):
                        up_unit(G_MLP + 8 * c + g, u)
                with pe.Fori(0, 4) as g:
                    down(c, g)


C_ITEMS = ((2, 3), (1,), (0,))
C_SPAN = ((OFF_K[2], 384), (OFF_K[1], 384), (OFF_K[0], 512))
C_BANK = (2, 1, 0)
C_BLOCKS_DONE = (2, 3, 4)


def b_lam(rows, i):
    return rows[:, 64 * i:64 * i + 64]


_INS = ["x", "w_in", "w_out", "g_attn", "g_mlp", "w_mlp_in", "w_mlp_out", "rel_bias_table",
        "diff_lam_q1", "diff_lam_k1", "diff_lam_q2", "diff_lam_k2", "diff_subln_g", "g_final"]


def kernel(**inputs):
    import numpy as np
    import concourse.bacc as bacc
    from concourse.bass_utils import run_bass_kernel_spmd

    nc = bacc.Bacc("TRN2", target_bir_lowering=False, num_devices=1,
                   dynamic_dma_scratch_size=1024)
    arrays, args = {}, []
    for name in _INS:
        a = np.ascontiguousarray(inputs[name])
        arrays[f"in_{name}"] = a
        args.append(nc.dram_tensor(f"in_{name}", a.shape, mybir.dt.from_np(a.dtype), kind="ExternalInput").ap())
    args.append(nc.dram_tensor("out_0", (1, SEQ, D), F32, kind="ExternalOutput").ap())
    build(nc, *args)
    r = run_bass_kernel_spmd(nc, [arrays], core_ids=[0])
    return r.results[0]["out_0"]
```

```python
import math
from contextlib import ExitStack

import concourse.bass as bass
from concourse import mybir

F32 = mybir.dt.float32
F32R = mybir.dt.float32r
ACT = mybir.ActivationFunctionType
ALU = mybir.AluOpType
AX_X = mybir.AxisListType.X

P = 128
SEQ = 512
D = 2048
FF = 8192
NT = SEQ // P
NK = D // P
HEADS_A, HEADS_B, HEADS_C = 6, 4, 6
HEADS = HEADS_A + HEADS_B + HEADS_C
GA, GB, GC = 1, 1 + HEADS_A, 1 + HEADS_A + HEADS_B
G_OUT = HEADS
G_MLP = G_OUT + D // 512
CHUNKS = 4
UNIT_W = 512
HEAD_W = 3 * P
AHEAD = 3
SPLIT_RING = 4
EPS = 1e-6
NORM_SLOTS = [[3], [4], [5], [6, 7], [8], [9], [10, 11], [12], [13], [14, 15]] + [[]] * 6
X_CHUNKS = [(0, 128), (128, 512), (512, 1024), (1024, 1536), (1536, 2048)]
G_LAST = G_MLP + 8 * CHUNKS - 1
MASKED = -1e30
NUM_BUCKETS, MAX_DISTANCE = 32, 2048
SCALE_AC = 1.0 / math.sqrt(P)
SCALE_B = 1.0 / math.sqrt(P // 2)
LAM_INIT = 0.8 - 0.6 * math.exp(0.0)
VEC = SEQ + P

OFF_Q = [0, 128, 384, 768]
OFF_K = [0, 512, 896, 1152]
PACKED = 1280


def bucket_runs():
    import numpy as np

    half = NUM_BUCKETS // 2
    dist = np.arange(SEQ)
    nf = np.maximum(dist, half).astype(np.float32)
    large = half + (np.log(nf / np.float32(half)) / np.float32(math.log(MAX_DISTANCE / half))
                    * np.float32(NUM_BUCKETS - half)).astype(np.int32)
    bucket = np.where(dist < half, dist, np.minimum(large, NUM_BUCKETS - 1))
    return [(int(b), int(dist[bucket == b][0]), int(dist[bucket == b][-1])) for b in np.unique(bucket)]


VEC_STEPS = 10 + len(bucket_runs())


def build(nc, x, w_in, w_out, g_attn, g_mlp, w_up, w_down, table, lq1, lk1, lq2, lk2, g_sub, g_final, out):
    ctx = ExitStack()
    with ctx:
        def sb(name, shape, dtype=F32):
            return ctx.enter_context(nc.sbuf_tensor(name, shape, dtype))

        def sem(name):
            return ctx.enter_context(nc.semaphore(name))

        raw = sb("raw", [P, 8, UNIT_W])
        w_hi = sb("w_hi", [P, SPLIT_RING, UNIT_W], F32R)
        w_lo = sb("w_lo", [P, SPLIT_RING, UNIT_W], F32R)
        h_hi = sb("h_hi", [P, NK, SEQ], F32R)
        h_lo = sb("h_lo", [P, NK, SEQ], F32R)
        m_hi = sb("m_hi", [P, NK, SEQ], F32R)
        m_lo = sb("m_lo", [P, NK, SEQ], F32R)
        res = sb("res", [P, NT, D])
        flat = res[:, :, :].rearrange("p t c -> p (t c)")
        bias = flat[:, 0:10 * SEQ].rearrange("p (h c) -> p h c", h=10)
        b_out = flat[:, 7168:7680]
        b_sq = flat[:, 7680:8192]
        attn = sb("attn", [P, 2 * PACKED])
        map0, map1 = attn[:, 0:PACKED], attn[:, PACKED:2 * PACKED]
        q_t, k_t = map0[:, 0:SEQ], map0[:, SEQ:2 * SEQ]
        v_t = map1[:, 0:SEQ]
        relu_s = attn[:, 0:4 * SEQ].rearrange("p (b i) -> p b i", b=4)
        g_fin = attn[:, 0:D]
        v_hi = sb("v_hi", [P, SEQ], F32R)
        v_lo = sb("v_lo", [P, SEQ], F32R)
        scratch = sb("scratch", [P, SEQ])
        rstd = sb("rstd", [P, SEQ])
        u_hi = sb("u_hi", [P, PACKED], F32R)
        u_lo = sb("u_lo", [P, PACKED], F32R)
        ident = sb("ident", [P, P])
        ones_r = sb("ones_r", [P, P], F32R)
        ones = ones_r[:, :].bitcast(F32)
        tri_r = sb("tri_r", [P, P], F32R)
        keep = sb("keep", [P, P])
        drop = sb("drop", [P, P])
        small = sb("small", [P, 72])
        ga_col, gm_col = small[:, 0:16], small[:, 16:32]
        gs_col = small[:, 32:33]
        eps_c = small[:, 33:34]
        neg_lam = small[:, 34:35]
        lam_s = small[:, 36:40]
        mx = small[:, 40:48]
        nm = small[:, 48:56]
        sums = small[:, 56:64]
        rec = small[:, 64:72]
        parts = small[:, 56:72]
        sq_sum = map1[:, PACKED - SEQ:PACKED]
        sq_pair = [rstd[:, :], scratch[:, :]]
        late_sq = [scratch[:, :], sq_sum]
        q_hi, q_lo = m_hi[:, NK - 1, :], m_lo[:, NK - 1, :]

        def k_of(head_is_last):
            return (h_hi[:, 0, :], h_lo[:, 0, :]) if head_is_last else (m_hi[:, NK - 2, :], m_lo[:, NK - 2, :])

        def packed_blocks(t, b):
            for k in range(0, b + 1, 2):
                n = min(2, b + 1 - k)
                o = OFF_K[k] + (b - k) * P
                if n == 2:
                    step = OFF_K[k + 1] - OFF_K[k] - P
                    yield k, n, t[:, o:o + 2 * step].rearrange("p (k i) -> p k i", k=2)[:, :, 0:P]
                else:
                    yield k, n, t[:, o:o + P].rearrange("p (k i) -> p k i", k=1)

        vec = map0[0:10, P:P + VEC + NUM_BUCKETS + 1]
        g_rows = map1[0:33, 512:512 + P]
        tab_rows = map1[0:NUM_BUCKETS, 640:650]
        bank = [ctx.enter_context(nc.psum_tensor(f"bank{i}", [P, 512], F32)) for i in range(8)]
        acc = bank[0:4]
        att = bank[4:8]
        tr_bank = [bank[6], bank[3]]
        bias_rows = nc.dram_tensor("bias_rows", [10, P, VEC], F32, kind="Internal")

        s_x = [sem(f"x_chunk{c}_loaded") for c in range(len(X_CHUNKS))]
        s_garow = sem("first_norm_weights_loaded")
        s_rowsl = sem("small_rows_loaded")
        s_colT = sem("small_rows_transposed")
        s_small = sem("norm_weights_by_feature")
        s_lamv = sem("lambda_vectors_loaded")
        s_const = sem("constants_made")
        s_tri = sem("triangle_rounded")
        s_raw = [sem(f"raw_quad_slot{i}_loaded") for i in range(2)]
        s_hi = sem("unit_hi_made")
        s_lo = sem("unit_lo_made")
        s_unit = sem("unit_multiplied")
        s_acc = sem("acc_bank_finished_but_the_last")
        s_evac = sem("acc_bank_read")
        s_xt = sem("x_transposed")
        s_hhi = sem("h_hi_made")
        s_sq = sem("square_made")
        s_hlo = sem("h_lo_made")
        s_sqsum = sem("square_added")
        s_ssq = sem("sum_of_squares_in_psum")
        s_root = sem("root_made")
        s_rstd = sem("rstd_made")
        s_tab = sem("bias_table_loaded")
        s_vecb = sem("bias_vector_step")
        s_rows = sem("bias_rows_stored")
        s_bias = sem("bias_loaded")
        s_lam = sem("lambda_step")
        s_lame = sem("lambda_exps")
        s_qkh = sem("q_k_hi_made")
        s_qkl = sem("q_k_lo_made")
        s_vt = sem("v_transposed")
        s_v = sem("v_hi_made")
        s_vl = sem("v_lo_made")
        s_aS, s_bS = sem("a_scores"), sem("b_scores")
        s_aL, s_bL = sem("a_logits"), sem("b_logits")
        s_mx = sem("row_max")
        s_nm = sem("negated_max")
        s_e = sem("exps")
        s_r = sem("reciprocal_sums")
        s_rl = sem("second_map_weight")
        s_p0 = sem("first_map_scaled")
        s_p = sem("probs_ready")
        s_pt = sem("probs_transposed")
        s_ptc = sem("probs_transposed_hi")
        s_ptl = sem("probs_transposed_lo")
        s_o = sem("head_out_in_psum")
        s_bo = sem("b_out_copied")
        s_bssq = sem("b_sum_of_squares")
        s_bln = sem("b_log")
        s_broot = sem("b_reciprocal_root")
        s_bn = sem("b_normed")
        s_z = sem("c_scores")
        s_zc = sem("c_logits_copied")
        s_zl = sem("c_log_step")
        s_sp = sem("c_softplus")
        s_spm = sem("c_softplus_masked")
        s_uh = sem("c_softplus_hi")
        s_ul = sem("c_softplus_lo")
        s_rs = sem("c_sums_in_psum")
        s_d = sem("c_exponent")
        s_ca = sem("c_exp")
        s_cah = sem("c_probs_hi")
        s_cal = sem("c_probs_lo")
        s_dm = sem("c_exponent_masked")
        s_mh = sem("mixed_hi_made")
        s_mix = sem("mixed_lo_made")
        s_res = sem("residual_loaded")
        s_rsc = sem("relu_scaled")
        s_rsq = sem("relu_squared")
        s_uhh = sem("hidden_hi_made")
        s_hid = sem("hidden_lo_made")
        s_gfin = sem("g_final_loaded")
        s_fsq = sem("final_squares_summed")
        s_ftot = sem("final_sum_of_squares")
        s_froot = sem("final_root")
        s_frec = sem("final_reciprocal")
        s_fg = sem("final_times_g")
        s_fina = sem("final_first_columns_ready")
        s_finb = sem("final_last_columns_ready")
        s_out = sem("out_stored")

        def raw_loaded(G, u, after_heads):
            quads = 2 * G + (u // 4) // 2 + 1
            return 16 * quads + 32 * 2 * HEADS if after_heads else 48 * quads

        def banks_done(G, b, after_heads):
            return 4 * G - HEADS + b + 1 if after_heads else 3 * G + b + 1

        def wait_bank(engine, G, b, after_heads):
            if b == (3 if after_heads else 2):
                engine.wait_ge(s_unit, 16 * G + 16)
            else:
                engine.wait_ge(s_acc, 3 * G - HEADS + b + 1 if after_heads else 2 * G + b + 1)

        block = ctx.enter_context(nc.Block())

        @block.sync
        def _(sp):
            x_v = x[0].rearrange("(t p) c -> p t c", p=P)
            in_v = w_in[0].rearrange("(k p) c -> p k c", p=P)
            out_v = w_out[0].rearrange("(k p) c -> p k c", p=P)
            up_v = w_up[0].rearrange("(k p) c -> p k c", p=P)
            down_v = w_down[0].rearrange("(k p) c -> p k c", p=P)
            def load_x(c):
                a, b = X_CHUNKS[c]
                sp.dma_start(res[:, :, a:b], x_v[:, :, a:b]).then_inc(s_x[c], 16)

            load_x(0)

            def slot_free(G, q):
                sp.wait_ge(s_lo, 16 * G + 4 * q - 4)

            def load_head(G, q, base, heads, h):
                for part in range(3):
                    cols = bass.ds(base + part * heads * P + h * P, P)
                    sp.dma_start(raw[:, 4 * (q % 2):4 * (q % 2) + 4, part * P:part * P + P],
                                 in_v[:, 4 * q:4 * q + 4, cols]).then_inc(s_raw[q % 2], 16)

            for q in range(4):
                if q >= 2:
                    slot_free(0, q)
                load_head(0, q, 0, HEADS_A, 0)
                if q == 0:
                    load_x(1)
                    sp.dma_start(g_rows[16:32, :], g_mlp[0].rearrange("(k p) -> k p", p=P)).then_inc(s_rowsl, 16)
                    sp.dma_start(g_rows[32:33, :], g_sub).then_inc(s_rowsl, 16)
                    sp.dma_start(tab_rows, table).then_inc(s_rowsl, 16)
                    load_x(2)
                if q == 1:
                    load_x(3)
                    load_x(4)
                    for i, v in enumerate((lq1, lk1, lq2, lk2)):
                        sp.dma_start(b_lam(map1, i), v.to_broadcast([P, P // 2])).then_inc(s_lamv, 16)
                    sp.wait_ge(s_vecb, VEC_STEPS)
                    value = vec[:, 0:VEC].rearrange("h (r n) -> h r n", r=1)
                    sp.dma_start(bias_rows.ap(), value.to_broadcast([10, P, VEC])).then_inc(s_rows, 16)
            for q in range(4):
                slot_free(1, q)
                load_head(1, q, 0, HEADS_A, 1)
                if q == 0:
                    sp.wait_ge(s_rows, 16)
                    sp.wait_ge(s_xt, NK)
                    skewed = bass.AP(tensor=bias_rows, offset=P - 1, ap=[[VEC - 1, P], [P * VEC, 10], [1, SEQ]])
                    sp.dma_start(bias, skewed).then_inc(s_bias, 16)
            with sp.Fori(2, HEADS_A) as h:
                for q in range(4):
                    slot_free(h, q)
                    load_head(h, q, 0, HEADS_A, h)
            with sp.Fori(0, HEADS_B) as h:
                for q in range(4):
                    slot_free(HEADS_A + h, q)
                    load_head(HEADS_A + h, q, 3 * HEADS_A * P, HEADS_B, h)
            first_c = HEADS_A + HEADS_B
            for q in range(4):
                slot_free(first_c, q)
                load_head(first_c, q, 3 * first_c * P, HEADS_C, 0)
            for q in range(4):
                slot_free(first_c + 1, q)
                load_head(first_c + 1, q, 3 * first_c * P, HEADS_C, 1)
            sp.wait_ge(s_mix, first_c)
            sp.dma_start(res[:, :, :], x_v).then_inc(s_res, 16)
            with sp.Fori(2, HEADS_C) as h:
                for q in range(4):
                    slot_free(first_c + h, q)
                    load_head(first_c + h, q, 3 * first_c * P, HEADS_C, h)
            with sp.Fori(0, 4) as g:
                for q in range(4):
                    slot_free(G_OUT + g, q)
                    sp.dma_start(raw[:, 4 * (q % 2):4 * (q % 2) + 4, :],
                                 out_v[:, 4 * q:4 * q + 4, bass.ds(512 * g, 512)]).then_inc(s_raw[q % 2], 16)
            def load_up(c, g):
                for q in range(4):
                    slot_free(G_MLP + 8 * c + g, q)
                    sp.dma_start(raw[:, 4 * (q % 2):4 * (q % 2) + 4, :],
                                 up_v[:, 4 * q:4 * q + 4, bass.ds(2048 * c + 512 * g, 512)])\
                        .then_inc(s_raw[q % 2], 16)

            def load_down(c, g):
                for q in range(4):
                    slot_free(G_MLP + 8 * c + 4 + g, q)
                    sp.dma_start(raw[:, 4 * (q % 2):4 * (q % 2) + 4, :],
                                 down_v[:, bass.ds(NK * c + 4 * q, 4), bass.ds(512 * g, 512)])\
                        .then_inc(s_raw[q % 2], 16)

            with sp.Fori(0, CHUNKS - 1) as c:
                with sp.Fori(0, 4) as g:
                    load_up(c, g)
                with sp.Fori(0, 4) as g:
                    load_down(c, g)
            with sp.Fori(0, 4) as g:
                load_up(CHUNKS - 1, g)
            load_down(CHUNKS - 1, 0)
            sp.wait_ge(s_hid, NK * CHUNKS)
            sp.dma_start(g_fin, g_final.rearrange("(o c) -> o c", o=1).to_broadcast([P, D])).then_inc(s_gfin, 16)
            with sp.Fori(1, 4) as g:
                load_down(CHUNKS - 1, g)
            out_t = out[0].rearrange("(t p) c -> p t c", p=P)
            for t in range(NT):
                sp.wait_ge(s_finb, t + 1)
                sp.dma_start(out_t[:, t, D - 512:D], res[:, t, D - 512:D]).then_inc(s_out, 16)
                for i in range(2):
                    sp.wait_ge(s_fina, 2 * t + i + 1)
                    cols = slice(768 * i, 768 * i + 768)
                    sp.dma_start(out_t[:, t, cols], res[:, t, cols]).then_inc(s_out, 16)
            sp.wait_ge(s_out, 48 * NT)

        @block.gpsimd
        def _(pool):
            nc.gpsimd.memset(ident[:, :], 0.0).then_inc(s_const, 1)
            nc.gpsimd.memset(ones, 1.0).then_inc(s_const, 1)
            nc.gpsimd.memset(eps_c, EPS).then_inc(s_const, 1)
            pool.wait_ge(s_const, 3)
            nc.gpsimd.affine_select(out=ident[:, :], in_=ident[:, :], compare_op=ALU.not_equal, fill=1.0,
                                    base=0, pattern=[[-1, P]], channel_multiplier=1).then_inc(s_const, 1)
            nc.gpsimd.affine_select(out=map0[:, 0:P], in_=ones[:, :], compare_op=ALU.is_ge, fill=0.0,
                                    base=0, pattern=[[-1, P]], channel_multiplier=1).then_inc(s_const, 1)

            nc.gpsimd.affine_select(out=keep[:, :], in_=ones[:, :], compare_op=ALU.is_gt, fill=0.0,
                                    base=0, pattern=[[1, P]], channel_multiplier=-1).then_inc(s_const, 1)
            nc.gpsimd.memset(drop[:, :], 0.0).then_inc(s_const, 1)
            pool.wait_ge(s_const, 7)
            nc.gpsimd.affine_select(out=drop[:, :], in_=drop[:, :], compare_op=ALU.is_gt, fill=MASKED,
                                    base=0, pattern=[[1, P]], channel_multiplier=-1).then_inc(s_const, 1)

            def add_squares(first):
                for n in range(first, first + NK):
                    pool.wait_ge(s_sq, n + 1)
                    if n == first:
                        nc.gpsimd.tensor_copy(sq_sum[:, :], sq_pair[n % 2]).then_inc(s_sqsum, 1)
                    else:
                        pool.wait_ge(s_sqsum, n)
                        nc.gpsimd.tensor_tensor(sq_sum[:, :], sq_sum[:, :], sq_pair[n % 2], ALU.add)\
                            .then_inc(s_sqsum, 1)

            add_squares(0)

            def mask_c(h):
                def softplus_mask(s):
                    for b in C_ITEMS[s]:
                        d = map1[:, OFF_K[b]:OFF_K[b] + P]
                        pool.wait_ge(s_sp, 3 * h + s + 1)
                        nc.gpsimd.tensor_tensor(d, d, keep[:, :], ALU.mult).then_inc(s_spm, 1)

                def exponent_mask(s):
                    for b in C_ITEMS[s]:
                        d = map0[:, OFF_K[b]:OFF_K[b] + P]
                        pool.wait_ge(s_d, 3 * h + s + 1)
                        nc.gpsimd.tensor_tensor(d, d, drop[:, :], ALU.add).then_inc(s_dm, 1)

                softplus_mask(0)
                softplus_mask(1)
                softplus_mask(2)
                exponent_mask(0)
                exponent_mask(1)
                exponent_mask(2)

            pool.wait_ge(s_const, 8)
            with pool.Fori(0, HEADS_C) as h:
                mask_c(h)
            add_squares(NK)

        @block.scalar
        def _(act):
            def split(G, u, width, after_heads):
                if u % 4 == 0:
                    act.wait_ge(s_raw[(u // 4) % 2], raw_loaded(G, u, after_heads))
                if not (isinstance(G, int) and 16 * G + u < SPLIT_RING):
                    act.wait_ge(s_unit, 16 * G + u - SPLIT_RING + 1)
                nc.scalar.activation(w_hi[:, u % SPLIT_RING, 0:width], raw[:, u % 8, 0:width],
                                     ACT.Copy).then_inc(s_hi, 1)

            def split_kept(u):
                if u % 4 == 0:
                    act.wait_ge(s_raw[(u // 4) % 2], raw_loaded(G_LAST, u, True))
                nc.scalar.activation(h_hi[:, u, :], raw[:, u % 8, :], ACT.Copy).then_inc(s_hi, 1)

            def norm_block(n, g_col):
                k = n % NK
                act.wait_ge(s_xt, n + 1)
                nc.scalar.activation(h_hi[:, k, :], att[n % 4][:, :], ACT.Copy, scale=g_col[:, k:k + 1])\
                    .then_inc(s_hhi, 1)
                if n % NK >= 2:
                    act.wait_ge(s_sqsum, n - 1)
                nc.scalar.activation(sq_pair[n % 2], att[n % 4][:, :], ACT.Square).then_inc(s_sq, 1)

            def norm_root(n):
                act.wait_ge(s_ssq, n + 1)
                nc.scalar.activation(rstd[:, :], att[3][:, :], ACT.Sqrt, bias=eps_c, scale=1.0 / D)\
                    .then_inc(s_root, 1)

            act.dma_start(g_rows[0:16, :], g_attn[0].rearrange("(k p) -> k p", p=P)).then_inc(s_garow, 16)
            nc.scalar.preload_act_table_set("natural_log_exp_and_others")
            act.wait_ge(s_colT, 1)
            nc.scalar.activation(ga_col, att[3][:, 0:16], ACT.Copy).then_inc(s_small, 1)
            act.wait_ge(s_small, 1)
            for u in range(AHEAD):
                norm_block(u, ga_col)
                split(0, u, HEAD_W, False)
            act.wait_ge(s_colT, 2)
            nc.scalar.activation(vec[:, VEC:VEC + NUM_BUCKETS], att[3][0:10, 64:64 + NUM_BUCKETS], ACT.Copy)\
                .then_inc(s_tab, 1)
            nc.scalar.activation(small[:, 16:33], att[3][:, 16:33], ACT.Copy).then_inc(s_small, 1)
            act.wait_ge(s_const, 5)
            nc.scalar.activation(tri_r[:, :], map0[:, 0:P], ACT.Copy).then_inc(s_tri, 1)

            def head_hi(head, is_last=False):
                for i, (src, dst) in enumerate(((q_t, q_hi), (k_t, k_of(is_last)[0]))):
                    act.wait_ge(s_evac, 3 * head + i + 1)
                    nc.scalar.activation(dst, src, ACT.Copy).then_inc(s_qkh, 1)

            for u in range(NK):
                for n in NORM_SLOTS[u]:
                    norm_block(n, ga_col)
                split(0, u + AHEAD, HEAD_W, False)
                if u == 11:
                    act.wait_ge(s_small, 2)
                    act.wait_ge(s_lam, 4)
                    nc.scalar.activation(lam_s[:, 2:4], lam_s[:, 0:2], ACT.Exp).then_inc(s_lame, 1)
                if u == 12:
                    norm_root(0)
            nc.scalar.preload_act_table_set("natural_log_exp_and_others")
            head_hi(0)

            def copy_v(head):
                act.wait_ge(s_vt, head + 1)
                nc.scalar.activation(v_hi[:, :], att[3][:, :], ACT.Copy).then_inc(s_v, 1)

            def copy_probs(count, b):
                act.wait_ge(s_pt, count)
                for k, n, dst in packed_blocks(u_hi, b):
                    last = nc.scalar.activation(dst, tr_bank[b % 2][:, P * k:P * (k + n)]
                                                .rearrange("p (k i) -> p k i", i=P), ACT.Copy)
                last.then_inc(s_ptc, 1)

            def exp_rows(count, b, m, scale):
                rows = (map0, map1)[m][:, OFF_Q[b]:OFF_Q[b] + P * (b + 1)]
                c = 2 * b + m
                act.wait_ge(s_nm, count)
                nc.scalar.activation(rows, rows, ACT.Exp, bias=nm[:, c:c + 1], scale=scale,
                                     accum_out=sums[:, c:c + 1]).then_inc(s_e, 1)

            with act.Fori(0, HEADS_A) as h:
                for u in range(NK):
                    split(GA + h, u + AHEAD, HEAD_W, False)
                    if u == 1:
                        copy_v(h)
                    if 1 <= u <= 4:
                        exp_rows(4 * h + u, u - 1, 0, SCALE_AC)
                    if u in (5, 6, 7, 9):
                        b = (5, 6, 7, 9).index(u)
                        copy_probs(4 * h + b + 1, b)
                head_hi(GA + h)
            with act.Fori(0, HEADS_B) as h:
                for u in range(NK):
                    split(GB + h, u + AHEAD, HEAD_W, False)
                    if u == 1:
                        copy_v(HEADS_A + h)
                    if u in (2, 4, 6, 8):
                        b = u // 2 - 1
                        for m in range(2):
                            exp_rows(4 * HEADS_A + 8 * h + 2 * b + m + 1, b, m, SCALE_B)
                    if u in (5, 7, 9, 11):
                        b = (u - 5) // 2
                        copy_probs(4 * (HEADS_A + h) + b + 1, b)
                    if u == 12:
                        act.wait_ge(s_o, HEADS_A + h + 1)
                        nc.scalar.activation(b_sq, att[3][:, :], ACT.Square).then_inc(s_bo, 1)
                        nc.scalar.activation(b_out, att[3][:, :], ACT.Copy).then_inc(s_bo, 1)
                    if u == 13:
                        act.wait_ge(s_bssq, h + 1)
                        nc.scalar.activation(b_sq, att[0][:, :], ACT.Ln, bias=eps_c, scale=1.0 / P)\
                            .then_inc(s_bln, 1)
                        act.wait_ge(s_bln, h + 1)
                        nc.scalar.activation(b_sq, b_sq, ACT.Exp, scale=-0.5).then_inc(s_broot, 1)
                head_hi(GB + h)

            def attend_c(u, h):
                if u == 1:
                    copy_v(HEADS_A + HEADS_B + h)
                if u in (1, 3, 5):
                    s = u // 2
                    lo, n = C_SPAN[s]
                    t = map1[:, lo:lo + n]
                    act.wait_ge(s_z, 3 * h + s + 1)
                    nc.scalar.activation(t, att[C_BANK[s]][:, 0:n], ACT.Abs, scale=SCALE_AC).then_inc(s_zl, 1)
                    nc.scalar.activation(map0[:, lo:lo + n], att[C_BANK[s]][:, 0:n], ACT.Copy,
                                         scale=SCALE_AC).then_inc(s_zc, 1)
                    act.wait_ge(s_zl, 9 * h + 3 * s + 1)
                    nc.scalar.activation(t, t, ACT.Exp, scale=-1.0).then_inc(s_zl, 1)
                    act.wait_ge(s_zl, 9 * h + 3 * s + 2)
                    nc.scalar.activation(t, t, ACT.Ln, bias=1.0).then_inc(s_zl, 1)
                if u in (8, 10, 12):
                    s = (u - 8) // 2
                    lo, n = C_SPAN[s]
                    act.wait_ge(s_dm, 4 * h + C_BLOCKS_DONE[s])
                    nc.scalar.activation(map1[:, lo:lo + n], map0[:, lo:lo + n], ACT.Exp).then_inc(s_ca, 1)
                for s in {11: (0,), 12: (1, 2)}.get(u, ()):
                    lo, n = C_SPAN[s]
                    act.wait_ge(s_rs, 3 * h + 3)
                    act.wait_ge(s_ca, 3 * h + s + 1)
                    nc.scalar.activation(u_hi[:, lo:lo + n], map1[:, lo:lo + n], ACT.Copy).then_inc(s_cah, 1)

            with act.Fori(0, HEADS_C - 2) as h:
                for u in range(NK):
                    split(GC + h, u + AHEAD, HEAD_W, False)
                    attend_c(u, h)
                head_hi(GC + h)
            for h in (HEADS_C - 2, HEADS_C - 1):
                for u in range(NK):
                    late = GC + h >= G_OUT or u + AHEAD >= NK
                    split(GC + h, u + AHEAD, UNIT_W if late else HEAD_W, late)
                    attend_c(u, h)
                if h == HEADS_C - 2:
                    head_hi(GC + h, is_last=True)
            for G in range(G_OUT + 1, G_MLP + 1):
                for u in range(NK):
                    split(G, u + AHEAD, UNIT_W, True)
                    if 1 <= u <= 4:
                        norm_block(NK + 4 * (G - G_OUT - 1) + u - 1, gm_col)
                    if G == G_MLP and u == 8:
                        norm_root(1)

            def relu_bank(G, b):
                wait_bank(act, G, b, True)
                nc.scalar.activation(relu_s[:, b, :], acc[b][:, :], ACT.Relu).then_inc(s_evac, 1)

            def up_tail(G):
                for b in range(4):
                    relu_bank(G, b)

            def square_block(c, g, b):
                first = 16 * c + 4 * g
                act.wait_ge(s_rsc, first + b + 1)
                if b >= 2:
                    act.wait_ge(s_hid, first + b - 1)
                nc.scalar.activation(late_sq[b % 2], relu_s[:, b, :], ACT.Square).then_inc(s_rsq, 1)

            def units(G, finish=None):
                for u in range(NK):
                    split(G, u + AHEAD, UNIT_W, True)
                    if finish is not None and u < 4:
                        square_block(*finish, u)

            up_tail(G_MLP)
            with act.Fori(1, 4) as g:
                units(G_MLP + g, (0, g - 1))
                up_tail(G_MLP + g)
            units(G_MLP + 4, (0, 3))
            with act.Fori(5, 8) as g:
                units(G_MLP + g)

            def chunk_up(c):
                units(G_MLP + 8 * c)
                up_tail(G_MLP + 8 * c)
                with act.Fori(1, 4) as g:
                    units(G_MLP + 8 * c + g, (c, g - 1))
                    up_tail(G_MLP + 8 * c + g)

            with act.Fori(1, CHUNKS - 1) as c:
                chunk_up(c)
                units(G_MLP + 8 * c + 4, (c, 3))
                with act.Fori(5, 8) as g:
                    units(G_MLP + 8 * c + g)
            c = CHUNKS - 1
            chunk_up(c)

            def square_piece(t, g):
                act.wait_ge(s_evac, banks_done(G_LAST - 3 + g, t, True))
                if 4 * g + t >= 2:
                    act.wait_ge(s_fsq, 4 * g + t - 1)
                nc.scalar.activation(late_sq[t % 2], res[:, t, 512 * g:512 * g + 512], ACT.Square,
                                     accum_out=parts[:, 4 * t + g:4 * t + g + 1]).then_inc(s_fsq, 1)

            for g in range(3):
                G = G_LAST - 3 + g
                for u in range(NK):
                    if G == G_LAST - 1 and u + AHEAD >= NK:
                        split_kept(u + AHEAD - NK)
                    else:
                        split(G, u + AHEAD, UNIT_W, True)
                    if g == 0 and u < 4:
                        square_block(c, 3, u)
                    if g > 0 and 4 <= u < 8:
                        square_piece(u - 4, g - 1)
            nc.scalar.preload_act_table(ACT.Sqrt)
            for u in range(AHEAD, NK):
                split_kept(u)
                if u in (6, 8, 10, 12):
                    square_piece((u - 6) // 2, 2)
            for t in range(NT):
                square_piece(t, 3)
                act.wait_ge(s_ftot, t + 1)
                nc.scalar.activation(nm[:, t:t + 1], mx[:, t:t + 1], ACT.Sqrt, bias=eps_c, scale=1.0 / D)\
                    .then_inc(s_froot, 1)
                act.wait_ge(s_frec, t + 1)
                act.wait_ge(s_fg, 4 * 3)
                for i in range(2):
                    r = res[:, t, 768 * i:768 * i + 768]
                    nc.scalar.activation(r, r, ACT.Copy, scale=nm[:, 4 + t:5 + t]).then_inc(s_fina, 1)

        @block.vector
        def _(dve):
            def split(G, u, width):
                dve.wait_ge(s_hi, 16 * G + u + 1)
                nc.vector.tensor_tensor(w_lo[:, u % SPLIT_RING, 0:width], raw[:, u % 8, 0:width],
                                        w_hi[:, u % SPLIT_RING, 0:width].bitcast(F32), ALU.subtract)\
                    .then_inc(s_lo, 1)

            def split_kept(u):
                dve.wait_ge(s_hi, 16 * G_LAST + u + 1)
                nc.vector.tensor_tensor(h_lo[:, u, :], raw[:, u % 8, :], h_hi[:, u, :].bitcast(F32),
                                        ALU.subtract).then_inc(s_lo, 1)

            def norm_block(n, g_col):
                k = n % NK
                dve.wait_ge(s_sq, n + 1)
                nc.vector.scalar_tensor_tensor(h_lo[:, k, :], att[n % 4][:, :], g_col[:, k:k + 1],
                                               h_hi[:, k, :].bitcast(F32), ALU.mult, ALU.subtract)\
                    .then_inc(s_hlo, 1)

            def norm_rstd(n):
                dve.wait_ge(s_root, n + 1)
                nc.vector.reciprocal(rstd[:, :], rstd[:, :]).then_inc(s_rstd, 1)

            def read_head(G, is_last=False):
                for b, dst in enumerate((q_t, k_t, v_t)):
                    wait_bank(dve, G, b, False)
                    nc.vector.tensor_tensor(dst, acc[b][:, :], rstd[:, :], ALU.mult).then_inc(s_evac, 1)
                k_hi, k_lo = k_of(is_last)
                for i, (src, hi, lo) in enumerate(((q_t, q_hi, q_lo), (k_t, k_hi, k_lo))):
                    dve.wait_ge(s_qkh, 2 * G + i + 1)
                    nc.vector.tensor_tensor(lo, src, hi.bitcast(F32), ALU.subtract).then_inc(s_qkl, 1)

            def v_low(head):
                dve.wait_ge(s_v, head + 1)
                nc.vector.tensor_tensor(v_lo[:, :], att[3][:, :], v_hi[:, :].bitcast(F32), ALU.subtract)\
                    .then_inc(s_vl, 1)

            def probs_low(head, b):
                dve.wait_ge(s_ptc, 4 * head + b + 1)
                for (k, n, dst), (_, _, hi) in zip(packed_blocks(u_lo, b), packed_blocks(u_hi, b)):
                    last = nc.vector.tensor_tensor(dst, tr_bank[b % 2][:, P * k:P * (k + n)]
                                                   .rearrange("p (k i) -> p k i", i=P), hi.bitcast(F32),
                                                   ALU.subtract)
                last.then_inc(s_ptl, 1)

            for u in range(AHEAD):
                norm_block(u, ga_col)
                split(0, u, HEAD_W)

            value = vec[:, 0:VEC]
            tab = vec[:, VEC:VEC + NUM_BUCKETS]
            inv = vec[:, VEC + NUM_BUCKETS:VEC + NUM_BUCKETS + 1]
            dve.wait_ge(s_tab, 1)
            nc.vector.memset(inv, 1.0 / SCALE_B).then_inc(s_vecb, 1)
            nc.vector.memset(value[:, SEQ:VEC], MASKED).then_inc(s_vecb, 1)
            dve.wait_ge(s_vecb, 2)
            nc.vector.memset(inv[0:HEADS_A, :], 1.0 / SCALE_AC).then_inc(s_vecb, 1)
            runs = bucket_runs()
            for b, lo, hi in runs:
                nc.vector.tensor_copy(value[:, SEQ - 1 - hi:SEQ - lo],
                                      tab[:, b:b + 1].to_broadcast([10, hi - lo + 1])).then_inc(s_vecb, 1)
            step = VEC_STEPS - 7

            def of_distance(first, last, by, rows=HEADS_A):
                a = SEQ - 1 - last
                return value[0:rows, a:SEQ - first:by]

            for first, last, by, add in ((0, 128, 4, math.log(2.0)), (0, 128, 16, math.log(3.0) - math.log(2.0)),
                                         (144, 496, 16, math.log(2.0))):
                dve.wait_ge(s_vecb, step)
                v = of_distance(first, last, by)
                nc.vector.tensor_scalar(v, v, add, None, ALU.add).then_inc(s_vecb, 1)
                step += 1
            dve.wait_ge(s_vecb, step)
            nc.vector.tensor_scalar(value[:, 0:SEQ], value[:, 0:SEQ], inv, None, ALU.mult).then_inc(s_vecb, 1)
            step += 1
            dve.wait_ge(s_vecb, step)
            for rest in (1, 2, 3):
                nc.vector.memset(of_distance(128 + rest, 508 + rest, 4), MASKED).then_inc(s_vecb, 1)
                step += 1
            assert step == VEC_STEPS

            def make_lambda(step):
                if step == 0:
                    dve.wait_ge(s_lamv, 64)
                    for i in range(2):
                        nc.vector.tensor_tensor(b_lam(map1, 2 * i), b_lam(map1, 2 * i), b_lam(map1, 2 * i + 1),
                                                ALU.mult).then_inc(s_lam, 1)
                if step == 1:
                    dve.wait_ge(s_lam, 2)
                    for i in range(2):
                        nc.vector.reduce_sum(lam_s[:, i:i + 1], b_lam(map1, 2 * i), AX_X).then_inc(s_lam, 1)
                if step == 2:
                    dve.wait_ge(s_lame, 1)
                    nc.vector.scalar_tensor_tensor(neg_lam, lam_s[:, 2:3], -1.0, lam_s[:, 3:4], ALU.mult, ALU.add)\
                        .then_inc(s_lam, 1)
                    dve.wait_ge(s_lam, 5)
                    nc.vector.tensor_scalar(neg_lam, neg_lam, -LAM_INIT, None, ALU.add).then_inc(s_lam, 1)
                    dve.wait_ge(s_small, 2)
                    nc.vector.tensor_scalar(gs_col, gs_col, 1.0 - LAM_INIT, None, ALU.mult).then_inc(s_lam, 1)

            for u in range(NK):
                for n in NORM_SLOTS[u]:
                    norm_block(n, ga_col)
                split(0, u + AHEAD, HEAD_W)
                if u in (10, 11, 12):
                    make_lambda(u - 10)
                if u == 13:
                    norm_rstd(0)
            dve.wait_ge(s_rstd, 1)
            dve.wait_ge(s_rows, 16)
            read_head(0)

            def logits(scores_sem, scores_count, logits_sem, head, b, m, psum):
                n = P * (b + 1)
                rows = (map0, map1)[m][:, OFF_Q[b]:OFF_Q[b] + n]
                c = 2 * b + m
                dve.wait_ge(scores_sem, scores_count)
                nc.vector.tensor_tensor(rows, psum[:, 0:n],
                                        bias[:, bass.ds(head, 1), SEQ - n:SEQ].rearrange("p o c -> p (o c)"),
                                        ALU.add).then_inc(logits_sem, 1)
                return rows, c

            def row_max(logits_sem, logits_count, rows, c, count, scale):
                dve.wait_ge(logits_sem, logits_count)
                nc.vector.reduce_max(mx[:, c:c + 1], rows, AX_X).then_inc(s_mx, 1)
                dve.wait_ge(s_mx, count)
                nc.vector.tensor_scalar(nm[:, c:c + 1], mx[:, c:c + 1], -scale, None, ALU.mult).then_inc(s_nm, 1)

            def mixed(head, src, count):
                hi = m_hi[:, bass.ds(head, 1), :].rearrange("p o c -> p (o c)")
                lo = m_lo[:, bass.ds(head, 1), :].rearrange("p o c -> p (o c)")
                nc.vector.tensor_scalar(hi, src, 1.0, None, ALU.mult).then_inc(s_mh, 1)
                dve.wait_ge(s_mh, count)
                nc.vector.tensor_tensor(lo, src, hi.bitcast(F32), ALU.subtract).then_inc(s_mix, 1)

            dve.wait_ge(s_bias, 16)
            with dve.Fori(0, HEADS_A) as h:
                for u in range(NK):
                    split(GA + h, u + AHEAD, HEAD_W)
                    if u in (5, 6, 7, 9):
                        probs_low(h, (5, 6, 7, 9).index(u))
                    if 1 <= u <= 4:
                        b = u - 1
                        rows, c = logits(s_aS, 4 * h + u, s_aL, h, b, 0, att[b % 2])
                        row_max(s_aL, 4 * h + u, rows, c, 4 * h + u, SCALE_AC)
                    if 2 <= u <= 5:
                        b = u - 2
                        dve.wait_ge(s_e, 4 * h + b + 1)
                        nc.vector.reciprocal(rec[:, 2 * b:2 * b + 1], sums[:, 2 * b:2 * b + 1]).then_inc(s_r, 1)
                        dve.wait_ge(s_r, 4 * h + b + 1)
                        rows = map0[:, OFF_Q[b]:OFF_Q[b] + P * (b + 1)]
                        nc.vector.tensor_scalar(rows, rows, rec[:, 2 * b:2 * b + 1], None, ALU.mult)\
                            .then_inc(s_p, 1)
                    if u == 3:
                        v_low(h)
                    if u == 11:
                        dve.wait_ge(s_o, h + 1)
                        mixed(h, att[3][:, :], h + 1)
                read_head(GA + h)
            with dve.Fori(0, HEADS_B) as h:
                n0 = 4 * HEADS_A + 8 * h
                for u in range(NK):
                    split(GB + h, u + AHEAD, HEAD_W)
                    if u == 2:
                        v_low(HEADS_A + h)
                    if u in (3, 5, 7, 9):
                        b = (u - 3) // 2
                        c = 2 * b
                        dve.wait_ge(s_e, n0 + 2 * b + 2)
                        nc.vector.reciprocal(rec[:, c:c + 2], sums[:, c:c + 2]).then_inc(s_r, 1)
                        dve.wait_ge(s_r, 4 * (HEADS_A + h) + b + 1)
                        rows0 = map0[:, OFF_Q[b]:OFF_Q[b] + P * (b + 1)]
                        rows1 = map1[:, OFF_Q[b]:OFF_Q[b] + P * (b + 1)]
                        nc.vector.tensor_scalar(rec[:, c + 1:c + 2], rec[:, c + 1:c + 2], neg_lam, None, ALU.mult)\
                            .then_inc(s_rl, 1)
                        nc.vector.tensor_scalar(rows0, rows0, rec[:, c:c + 1], None, ALU.mult).then_inc(s_p0, 1)
                        dve.wait_ge(s_rl, 4 * h + b + 1)
                        dve.wait_ge(s_p0, 4 * h + b + 1)
                        nc.vector.scalar_tensor_tensor(rows0, rows1, rec[:, c + 1:c + 2], rows0, ALU.mult, ALU.add)\
                            .then_inc(s_p, 1)
                    if u in (1, 3, 5, 7):
                        b = u // 2
                        pair = [logits(s_bS, 8 * h + 2 * b + m + 1, s_bL, HEADS_A + h, b, m, att[m])
                                for m in range(2)]
                        for m, (rows, c) in enumerate(pair):
                            row_max(s_bL, 8 * h + 2 * b + m + 1, rows, c, n0 + 2 * b + m + 1, SCALE_B)
                    if u in (6, 8, 10, 11):
                        probs_low(HEADS_A + h, (6, 8, 10, 11).index(u))
                    if u == 13:
                        dve.wait_ge(s_broot, h + 1)
                        nc.vector.scalar_tensor_tensor(b_out, b_out, gs_col, b_sq, ALU.mult, ALU.mult)\
                            .then_inc(s_bn, 1)
                        dve.wait_ge(s_bn, h + 1)
                        mixed(HEADS_A + h, b_out, HEADS_A + h + 1)
                read_head(GB + h)

            def attend_c(u, h, head):
                if u == 2:
                    v_low(head)
                for s in {11: (0,), 12: (1, 2)}.get(u, ()):
                    lo, n = C_SPAN[s]
                    dve.wait_ge(s_cah, 3 * h + s + 1)
                    nc.vector.tensor_tensor(u_lo[:, lo:lo + n], map1[:, lo:lo + n],
                                            u_hi[:, lo:lo + n].bitcast(F32), ALU.subtract).then_inc(s_cal, 1)
                if u in (3, 5, 7):
                    s = (u - 3) // 2
                    lo, n = C_SPAN[s]
                    dve.wait_ge(s_zl, 9 * h + 3 * s + 3)
                    dve.wait_ge(s_zc, 3 * h + s + 1)
                    nc.vector.scalar_tensor_tensor(map1[:, lo:lo + n], map0[:, lo:lo + n], 0.0, map1[:, lo:lo + n],
                                                   ALU.max, ALU.add).then_inc(s_sp, 1)
                if u in (4, 6, 8):
                    s = (u - 4) // 2
                    lo, n = C_SPAN[s]
                    dve.wait_ge(s_spm, 4 * h + C_BLOCKS_DONE[s])
                    nc.vector.tensor_scalar(u_hi[:, lo:lo + n], map1[:, lo:lo + n], 1.0, None, ALU.mult)\
                        .then_inc(s_uh, 1)
                    dve.wait_ge(s_uh, 3 * h + s + 1)
                    nc.vector.tensor_tensor(u_lo[:, lo:lo + n], map1[:, lo:lo + n],
                                            u_hi[:, lo:lo + n].bitcast(F32), ALU.subtract).then_inc(s_ul, 1)
                if u in (7, 9, 11):
                    s = (u - 7) // 2
                    lo, n = C_SPAN[s]
                    dve.wait_ge(s_rs, 3 * h + s + 1)
                    nc.vector.tensor_tensor(map0[:, lo:lo + n], map0[:, lo:lo + n], att[C_BANK[s]][:, 0:n],
                                            ALU.subtract).then_inc(s_d, 1)
                if u == 14:
                    dve.wait_ge(s_o, head + 1)
                    mixed(head, att[3][:, :], head + 1)

            with dve.Fori(0, HEADS_C - 2) as h:
                for u in range(NK):
                    split(GC + h, u + AHEAD, HEAD_W)
                    attend_c(u, h, HEADS_A + HEADS_B + h)
                read_head(GC + h)
            for h in (HEADS_C - 2, HEADS_C - 1):
                for u in range(NK):
                    late = GC + h >= G_OUT or u + AHEAD >= NK
                    split(GC + h, u + AHEAD, UNIT_W if late else HEAD_W)
                    attend_c(u, h, HEADS_A + HEADS_B + h)
                if h == HEADS_C - 2:
                    read_head(GC + h, is_last=True)

            def add_residual(G, g):
                for t in range(NT):
                    r = res[:, t, bass.ds(512 * g, 512)]
                    wait_bank(dve, G, t, True)
                    nc.vector.tensor_tensor(r, r, acc[t][:, :], ALU.add).then_inc(s_evac, 1)

            dve.wait_ge(s_res, 16)
            add_residual(G_OUT, 0)
            for G in range(G_OUT + 1, G_MLP + 1):
                for u in range(NK):
                    split(G, u + AHEAD, UNIT_W)
                    if 1 <= u <= 4:
                        norm_block(NK + 4 * (G - G_OUT - 1) + u - 1, gm_col)
                    if G == G_MLP and u == 9:
                        norm_rstd(1)
                if G < G_MLP:
                    add_residual(G, G - G_OUT)
            dve.wait_ge(s_rstd, 2)

            def up_tail(c, g):
                for b in range(4):
                    dve.wait_ge(s_evac, banks_done(G_MLP + 8 * c + g, b, True))
                    nc.vector.tensor_tensor(relu_s[:, b, :], relu_s[:, b, :], rstd[:, :], ALU.mult)\
                        .then_inc(s_rsc, 1)

            def hidden_block(c, g, b):
                first = 16 * c + 4 * g
                hi = m_hi[:, bass.ds(4 * g + b, 1), :].rearrange("p o c -> p (o c)")
                lo = m_lo[:, bass.ds(4 * g + b, 1), :].rearrange("p o c -> p (o c)")
                dve.wait_ge(s_rsc, first + b + 1)
                nc.vector.tensor_tensor(hi, relu_s[:, b, :], relu_s[:, b, :], ALU.mult).then_inc(s_uhh, 1)
                dve.wait_ge(s_uhh, first + b + 1)
                dve.wait_ge(s_rsq, first + b + 1)
                nc.vector.tensor_tensor(lo, late_sq[b % 2], hi.bitcast(F32), ALU.subtract)\
                    .then_inc(s_hid, 1)

            def units(G, finish=None):
                for u in range(NK):
                    split(G, u + AHEAD, UNIT_W)
                    if finish is not None and u < 4:
                        hidden_block(*finish, u)

            up_tail(0, 0)
            with dve.Fori(1, 4) as g:
                units(G_MLP + g, (0, g - 1))
                up_tail(0, g)
            units(G_MLP + 4, (0, 3))
            add_residual(G_MLP + 4, 0)
            with dve.Fori(1, 4) as g:
                units(G_MLP + 4 + g)
                add_residual(G_MLP + 4 + g, g)

            def chunk_up(c):
                units(G_MLP + 8 * c)
                up_tail(c, 0)
                with dve.Fori(1, 4) as g:
                    units(G_MLP + 8 * c + g, (c, g - 1))
                    up_tail(c, g)

            with dve.Fori(1, CHUNKS - 1) as c:
                chunk_up(c)
                units(G_MLP + 8 * c + 4, (c, 3))
                add_residual(G_MLP + 8 * c + 4, 0)
                with dve.Fori(1, 4) as g:
                    units(G_MLP + 8 * c + 4 + g)
                    add_residual(G_MLP + 8 * c + 4 + g, g)
            c = CHUNKS - 1
            chunk_up(c)

            def times_g(t, g):
                r = res[:, t, 512 * g:512 * g + 512]
                dve.wait_ge(s_fsq, 4 * g + t + 1)
                nc.vector.tensor_tensor(r, r, g_fin[:, 512 * g:512 * g + 512], ALU.mult).then_inc(s_fg, 1)

            for g in range(3):
                G = G_LAST - 3 + g
                for u in range(NK):
                    if G == G_LAST - 1 and u + AHEAD >= NK:
                        split_kept(u + AHEAD - NK)
                    else:
                        split(G, u + AHEAD, UNIT_W)
                    if g == 0 and u < 4:
                        hidden_block(c, 3, u)
                    if g > 0 and u == 8:
                        dve.wait_ge(s_gfin, 16)
                    if g > 0 and 8 <= u < 12:
                        times_g(u - 8, g - 1)
                add_residual(G, g)
            for u in range(AHEAD, NK):
                split_kept(u)
            for t in range(NT):
                times_g(t, 2)
            for t in range(NT):
                dve.wait_ge(s_acc, 3 * G_LAST - HEADS + t + 1)
                r = res[:, t, D - 512:D]
                nc.vector.tensor_tensor(r, r, acc[t][:, :], ALU.add).then_inc(s_evac, 1)
                dve.wait_ge(s_fsq, 12 + t + 1)
                nc.vector.reduce_sum(mx[:, t:t + 1], parts[:, 4 * t:4 * t + 4], AX_X).then_inc(s_ftot, 1)
                dve.wait_ge(s_froot, t + 1)
                nc.vector.reciprocal(nm[:, 4 + t:5 + t], nm[:, t:t + 1]).then_inc(s_frec, 1)
                dve.wait_ge(s_frec, t + 1)
                nc.vector.scalar_tensor_tensor(r, r, nm[:, 4 + t:5 + t], g_fin[:, D - 512:D], ALU.mult, ALU.mult)\
                    .then_inc(s_finb, 1)

        @block.tensor
        def _(pe):
            def mm(o, a, b, start, stop=True):
                return nc.tensor.matmul(o, a, b, start=start, stop=stop, skip_group_check=True)

            def mm3(o, a_hi, a_lo, b_hi, b_lo, start):
                mm(o, a_hi, b_hi, start=start)
                mm(o, a_hi, b_lo, start=False)
                return mm(o, a_lo, b_hi, start=False)

            def head_unit(G, u):
                s = u % SPLIT_RING
                pe.wait_ge(s_lo, 16 * G + u + 1)
                for b in range(3):
                    cols = slice(b * P, b * P + P)
                    if u == 0 and not (isinstance(G, int) and G == 0):
                        pe.wait_ge(s_evac, banks_done(G - 1, b, False))
                    mm(acc[b][:, :], w_hi[:, s, cols], h_hi[:, u, :], start=(u == 0))
                    mm(acc[b][:, :], w_hi[:, s, cols], h_lo[:, u, :], start=False)
                    last = mm(acc[b][:, :], w_lo[:, s, cols], h_hi[:, u, :], start=False)
                    if u == NK - 1 and b < 2:
                        last.then_inc(s_acc, 1)
                last.then_inc(s_unit, 1)

            def by_token_unit(G, u, prev_after_heads=True):
                s = u % SPLIT_RING
                pe.wait_ge(s_lo, 16 * G + u + 1)
                for t in range(NT):
                    toks = slice(t * P, t * P + P)
                    if u == 0:
                        if prev_after_heads:
                            pe.wait_ge(s_evac, banks_done(G - 1, t, True))
                        elif t < 3:
                            pe.wait_ge(s_evac, banks_done(G - 1, t, False))
                    mm(acc[t][:, :], m_hi[:, u, toks], w_hi[:, s, :], start=(u == 0))
                    mm(acc[t][:, :], m_hi[:, u, toks], w_lo[:, s, :], start=False)
                    last = mm(acc[t][:, :], m_lo[:, u, toks], w_hi[:, s, :], start=False)
                    if u == NK - 1 and t < 3:
                        last.then_inc(s_acc, 1)
                last.then_inc(s_unit, 1)

            def up_unit(G, u):
                s = u % SPLIT_RING
                pe.wait_ge(s_lo, 16 * G + u + 1)
                for b in range(4):
                    cols = slice(b * P, b * P + P)
                    if u == 0:
                        pe.wait_ge(s_evac, banks_done(G - 1, b, True))
                    mm(acc[b][:, :], w_hi[:, s, cols], h_hi[:, u, :], start=(u == 0))
                    mm(acc[b][:, :], w_hi[:, s, cols], h_lo[:, u, :], start=False)
                    last = mm(acc[b][:, :], w_lo[:, s, cols], h_hi[:, u, :], start=False)
                    if u == NK - 1 and b < 3:
                        last.then_inc(s_acc, 1)
                last.then_inc(s_unit, 1)

            def transpose_x(n):
                k = n % NK
                if n < NK and k in (0, 1, 4, 8, 12):
                    pe.wait_ge(s_x[(0, 1, 4, 8, 12).index(k)], 16)
                if n >= NK:
                    G = G_OUT + (n - NK) // 4
                    pe.wait_ge(s_evac, banks_done(G, 3, True))
                if n >= 4:
                    pe.wait_ge(s_hlo, n - 3)
                if n == 3:
                    pe.wait_ge(s_small, 2)
                for t in range(NT):
                    last = nc.tensor.transpose(att[n % 4][:, t * P:t * P + P], res[:, t, k * P:k * P + P],
                                               ident[:, :])
                last.then_inc(s_xt, 1)

            def sum_squares(n):
                pe.wait_ge(s_sqsum, NK * (n + 1))
                pe.wait_ge(s_hlo, NK * (n + 1))
                mm(att[3][:, :], ones[:, :], sq_sum[:, :], start=True).then_inc(s_ssq, 1)

            pe.wait_ge(s_const, 4)
            pe.wait_ge(s_garow, 16)
            nc.tensor.transpose(att[3][:, 0:16], g_rows[0:16, :], ident[0:16, 0:16]).then_inc(s_colT, 1)
            for n in range(AHEAD):
                transpose_x(n)
            pe.wait_ge(s_rowsl, 48)
            pe.wait_ge(s_small, 1)
            nc.tensor.transpose(att[3][:, 0:33], g_rows, ident[0:33, 0:33])
            nc.tensor.transpose(att[3][0:10, 64:64 + NUM_BUCKETS], tab_rows,
                                ident[0:NUM_BUCKETS, 0:NUM_BUCKETS]).then_inc(s_colT, 1)
            for u in range(NK):
                pe.wait_ge(s_hlo, u + 1)
                head_unit(0, u)
                for n in NORM_SLOTS[u]:
                    transpose_x(n)
                if u == 11:
                    sum_squares(0)

            def transpose_v(head):
                pe.wait_ge(s_evac, 3 * head + 3)
                for b in range(NT):
                    last = nc.tensor.transpose(att[3][:, b * P:b * P + P], v_t[:, b * P:b * P + P], ident[:, :])
                last.then_inc(s_vt, 1)

            def transpose_probs(head, b):
                pe.wait_ge(s_p, 4 * head + b + 1)
                if b >= 2:
                    pe.wait_ge(s_ptl, 4 * head + b - 1)
                for k in range(b + 1):
                    last = nc.tensor.transpose(tr_bank[b % 2][:, k * P:k * P + P],
                                               map0[:, OFF_Q[b] + k * P:OFF_Q[b] + k * P + P], ident[:, :])
                last.then_inc(s_pt, 1)

            def head_out(head):
                pe.wait_ge(s_vl, head + 1)
                for b in range(NT):
                    v, r = slice(b * P, b * P + P), slice(OFF_K[b], OFF_K[b] + SEQ - b * P)
                    last = mm3(att[3][:, b * P:SEQ], v_hi[:, v], v_lo[:, v], u_hi[:, r], u_lo[:, r], b == 0)
                last.then_inc(s_o, 1)

            k_hi, k_lo = k_of(False)
            with pe.Fori(0, HEADS_A) as h:
                for u in range(NK):
                    head_unit(GA + h, u)
                    if u == 0:
                        transpose_v(h)
                    if u <= 3:
                        if u >= 2:
                            pe.wait_ge(s_aL, 4 * h + u - 1)
                        rows, keys = slice(u * P, u * P + P), slice(0, P * (u + 1))
                        if u == 0:
                            pe.wait_ge(s_qkl, 2 * h + 2)
                        mm3(att[u % 2][:, keys], q_hi[:, rows], q_lo[:, rows], k_hi[:, keys], k_lo[:, keys],
                            True).then_inc(s_aS, 1)
                    if u in (4, 5, 6, 8):
                        transpose_probs(h, (4, 5, 6, 8).index(u))
                    if u == 10:
                        pe.wait_ge(s_ptl, 4 * h + 4)
                        head_out(h)
            with pe.Fori(0, HEADS_B) as h:
                for u in range(NK):
                    head_unit(GB + h, u)
                    if u == 0:
                        transpose_v(HEADS_A + h)
                    if u in (0, 2, 4, 6):
                        b = u // 2
                        for m in range(2):
                            if b >= 1:
                                pe.wait_ge(s_bL, 8 * h + 2 * b + m - 1)
                            half = slice(m * (P // 2), (m + 1) * (P // 2))
                            rows, keys = slice(b * P, b * P + P), slice(0, P * (b + 1))
                            if b == 0 and m == 0:
                                pe.wait_ge(s_qkl, 2 * (HEADS_A + h) + 2)
                            mm3(att[m][:, keys], q_hi[half, rows], q_lo[half, rows], k_hi[half, keys],
                                k_lo[half, keys], True).then_inc(s_bS, 1)
                    if u in (4, 6, 8, 10):
                        transpose_probs(HEADS_A + h, (u - 4) // 2)
                    if u == 11:
                        pe.wait_ge(s_ptl, 4 * (HEADS_A + h) + 4)
                        head_out(HEADS_A + h)
                    if u == 12:
                        pe.wait_ge(s_bo, 2 * h + 1)
                        mm(att[0][:, :], ones[:, :], b_sq, start=True).then_inc(s_bssq, 1)

            def attend_c(u, h, head):
                if u == 0:
                    transpose_v(head)
                    k_hi, k_lo = k_of(isinstance(h, int))
                    pe.wait_ge(s_qkl, 2 * head + 2)
                    for s, blocks in enumerate(C_ITEMS):
                        for j, b in enumerate(blocks):
                            o = OFF_K[b] - C_SPAN[s][0]
                            keys, rows = slice(b * P, b * P + P), slice(b * P, SEQ)
                            last = mm3(att[C_BANK[s]][:, o:o + SEQ - b * P], k_hi[:, keys], k_lo[:, keys],
                                       q_hi[:, rows], q_lo[:, rows], j == 0)
                        last.then_inc(s_z, 1)
                if u in (6, 8, 10):
                    s = (u - 6) // 2
                    pe.wait_ge(s_ul, 3 * h + s + 1)
                    first = True
                    for b in C_ITEMS[s]:
                        o = OFF_K[b] - C_SPAN[s][0]
                        for later in range(b, NT):
                            weight = tri_r if later == b else ones_r
                            skip = (later - b) * P
                            for part in (u_hi, u_lo):
                                last = mm(att[C_BANK[s]][:, o + skip:o + SEQ - b * P], weight[:, :],
                                          part[:, OFF_K[later]:OFF_K[later] + SEQ - later * P], start=first)
                                first = False
                    last.then_inc(s_rs, 1)
                if u == 13:
                    pe.wait_ge(s_cal, 3 * h + 3)
                    head_out(head)

            pe.wait_ge(s_tri, 1)
            with pe.Fori(0, HEADS_C - 1) as h:
                for u in range(NK):
                    head_unit(GC + h, u)
                    attend_c(u, h, HEADS_A + HEADS_B + h)
            for u in range(NK):
                if u == NK - 1:
                    pe.wait_ge(s_mix, HEADS)
                by_token_unit(G_OUT, u, prev_after_heads=False)
                attend_c(u, HEADS_C - 1, HEADS - 1)
            for G in range(G_OUT + 1, G_MLP):
                for u in range(NK):
                    by_token_unit(G, u)
                    if u < 4:
                        transpose_x(NK + 4 * (G - G_OUT - 1) + u)
            for u in range(NK):
                if u >= NK - 4:
                    pe.wait_ge(s_hlo, NK + u + 1)
                if u == 0:
                    pe.wait_ge(s_hlo, 2 * NK - 4)
                up_unit(G_MLP, u)
                if u < 4:
                    transpose_x(2 * NK - 4 + u)
                if u == 7:
                    sum_squares(1)
            with pe.Fori(1, 4) as g:
                for u in range(NK):
                    up_unit(G_MLP + g, u)

            def down(c, g):
                for u in range(NK):
                    if u % 4 == 0:
                        pe.wait_ge(s_hid, NK * c + u + 4)
                    by_token_unit(G_MLP + 8 * c + 4 + g, u)

            with pe.Fori(0, 4) as g:
                down(0, g)
            def up(c):
                with pe.Fori(0, 4) as g:
                    for u in range(NK):
                        up_unit(G_MLP + 8 * c + g, u)

            with pe.Fori(1, CHUNKS - 1) as c:
                up(c)
                with pe.Fori(0, 4) as g:
                    down(c, g)
            up(CHUNKS - 1)
            with pe.Fori(0, 3) as g:
                down(CHUNKS - 1, g)
            for tiles in ((0, 1), (2,), (3,)):
                for u in range(NK):
                    if tiles[0] == 0:
                        pe.wait_ge(s_lo, 16 * G_LAST + u + 1)
                    for t in tiles:
                        toks = slice(t * P, t * P + P)
                        if u == 0:
                            pe.wait_ge(s_evac, banks_done(G_LAST - 1, t, True))
                        mm(acc[t][:, :], m_hi[:, u, toks], h_hi[:, u, :], start=(u == 0))
                        mm(acc[t][:, :], m_hi[:, u, toks], h_lo[:, u, :], start=False)
                        last = mm(acc[t][:, :], m_lo[:, u, toks], h_hi[:, u, :], start=False)
                        if u == NK - 1:
                            last.then_inc(s_acc, 1)


C_ITEMS = ((2, 3), (1,), (0,))
C_SPAN = ((OFF_K[2], 384), (OFF_K[1], 384), (OFF_K[0], 512))
C_BANK = (2, 1, 0)
C_BLOCKS_DONE = (2, 3, 4)


def b_lam(rows, i):
    return rows[:, 64 * i:64 * i + 64]


_INS = ["x", "w_in", "w_out", "g_attn", "g_mlp", "w_mlp_in", "w_mlp_out", "rel_bias_table",
        "diff_lam_q1", "diff_lam_k1", "diff_lam_q2", "diff_lam_k2", "diff_subln_g", "g_final"]


def kernel(**inputs):
    import numpy as np
    import concourse.bacc as bacc
    from concourse.bass_utils import run_bass_kernel_spmd

    nc = bacc.Bacc("TRN2", target_bir_lowering=False, num_devices=1,
                   dynamic_dma_scratch_size=1024)
    arrays, args = {}, []
    for name in _INS:
        a = np.ascontiguousarray(inputs[name])
        arrays[f"in_{name}"] = a
        args.append(nc.dram_tensor(f"in_{name}", a.shape, mybir.dt.from_np(a.dtype), kind="ExternalInput").ap())
    args.append(nc.dram_tensor("out_0", (1, SEQ, D), F32, kind="ExternalOutput").ap())
    build(nc, *args)
    r = run_bass_kernel_spmd(nc, [arrays], core_ids=[0])
    return r.results[0]["out_0"]
```
